# Optimizing a Trainium2 kernel written in Bass

```python
import math, functools
import jax, jax.numpy as jnp
from jax import lax
import numpy as np
import math

D_MODEL = 1024
BATCH = 1
SEQ = 256
DEPTH = 1

GRID_W = 64
CTX_LEN = 256
HEAD_DIM = 64
A_HEADS = 8
A_KV_HEADS = 2
A_GROUP = A_HEADS // A_KV_HEADS
A_WIDTH = A_HEADS * HEAD_DIM
B_HEADS = 4
B_V_DIM = 2 * HEAD_DIM
B_WIDTH = B_HEADS * B_V_DIM
N_BRANCH = 2
A_Q_COLS = A_HEADS * HEAD_DIM
A_KV_COLS = A_KV_HEADS * HEAD_DIM
B_QK_COLS = B_HEADS * 2 * HEAD_DIM
IN_SPLIT = [A_Q_COLS, A_KV_COLS, A_KV_COLS, B_QK_COLS, B_QK_COLS, B_WIDTH, D_MODEL, D_MODEL]
IN_COLS = sum(IN_SPLIT)
IN_OFFSETS = [int(v) for v in np.cumsum(IN_SPLIT)[:-1]]
ROPE_THETA = 10000.0
AXIS_PAIRS = HEAD_DIM // 4
Q_BLOCK = 128
N_EXPERTS = 32
TOP_K = 4
D_EXPERT = D_MODEL
SWIGLU_LIMIT = 7.0
SWIGLU_ALPHA = 1.702
MOE_BLOCK = 128
N_MOD = 6
EPS = 1e-6
SUBLN_EPS = 1e-5


def _rmsnorm(x, gain, eps=EPS):
    xf = x.astype(jnp.float32)
    y = xf * lax.rsqrt(jnp.mean(xf * xf, axis=-1, keepdims=True) + eps)
    return (y * gain.astype(jnp.float32)).astype(x.dtype)

def _modulate(h, shift, scale):
    return h * (1 + scale) + shift

def _axial_rope(rows):
    row = jnp.repeat(jnp.arange(rows, dtype=jnp.float32), GRID_W)
    col = jnp.tile(jnp.arange(GRID_W, dtype=jnp.float32), rows)
    inv = 1.0 / (ROPE_THETA ** (jnp.arange(AXIS_PAIRS, dtype=jnp.float32) / AXIS_PAIRS))
    ang = jnp.concatenate([row[:, None] * inv, col[:, None] * inv], axis=-1)
    return jnp.cos(ang), jnp.sin(ang)

def _apply_rope(x, cos, sin):
    extra = x.ndim - 3
    cos = cos.reshape(cos.shape[0], *([1] * extra), cos.shape[1])
    sin = sin.reshape(sin.shape[0], *([1] * extra), sin.shape[1])
    xp = x.reshape(*x.shape[:-1], HEAD_DIM // 2, 2)
    x0, x1 = xp[..., 0], xp[..., 1]
    out = jnp.stack([x0 * cos - x1 * sin, x0 * sin + x1 * cos], axis=-1)
    return out.reshape(x.shape).astype(x.dtype)

def _project(h, w_in, q_norm_a, k_norm_a, q_norm_b, k_norm_b):
    b, n, _ = h.shape
    qa, ka, va, qb, kb, vb, ga, gb = jnp.split(h @ w_in, IN_OFFSETS, axis=-1)
    qa = _rmsnorm(qa.reshape(b, n, A_HEADS, HEAD_DIM), q_norm_a)
    ka = _rmsnorm(ka.reshape(b, n, A_KV_HEADS, HEAD_DIM), k_norm_a)
    va = va.reshape(b, n, A_KV_HEADS, HEAD_DIM)
    qb = _rmsnorm(qb.reshape(b, n, B_HEADS, 2, HEAD_DIM), q_norm_b)
    kb = _rmsnorm(kb.reshape(b, n, B_HEADS, 2, HEAD_DIM), k_norm_b)
    vb = vb.reshape(b, n, B_HEADS, B_V_DIM)
    return qa, ka, va, qb, kb, vb, ga, gb

def _gqa_attend(q, k, v):
    b, n = q.shape[:2]
    qg = q.reshape(b, n, A_KV_HEADS, A_GROUP, HEAD_DIM)
    s = jnp.einsum('bqhgd,bkhd->bhgqk', qg, k).astype(jnp.float32) * (HEAD_DIM ** -0.5)
    p = jax.nn.softmax(s, axis=-1).astype(v.dtype)
    o = jnp.einsum('bhgqk,bkhd->bqhgd', p, v)
    return o.reshape(b, n, A_WIDTH)

def _diff_attend(q, k, v, lam):
    s = jnp.einsum('bqhmd,bkhmd->bhmqk', q, k).astype(jnp.float32) * (HEAD_DIM ** -0.5)
    p = jax.nn.softmax(s, axis=-1)
    a = (p[:, :, 0] - lam * p[:, :, 1]).astype(v.dtype)
    return jnp.einsum('bhqk,bkhe->bqhe', a, v)

def _sweep_query_blocks(attend, q, k, v):
    b, s = q.shape[:2]
    nb = s // Q_BLOCK
    qb = jnp.moveaxis(q.reshape(b, nb, Q_BLOCK, *q.shape[2:]), 1, 0)
    o = lax.map(lambda qq: attend(qq, k, v), qb)
    o = jnp.moveaxis(o, 0, 1)
    return o.reshape(b, s, *o.shape[3:])

def _diff_out(o, subln, lam_init):
    o = _rmsnorm(o, subln, SUBLN_EPS) * (1.0 - lam_init)
    return o.reshape(o.shape[0], o.shape[1], B_WIDTH)

def _merge(ya, yb, ga, gb, w_oa, w_ob, w_out):
    merged = jax.nn.sigmoid(ga) * (ya @ w_oa) + jax.nn.sigmoid(gb) * (yb @ w_ob)
    return merged @ w_out

def _moe(h, router_w, router_b, w_gate, b_gate, w_up, b_up, w_down, b_down):
    t = h.shape[0]
    logits = (h @ router_w + router_b).astype(jnp.float32)
    top_logit, top_e = lax.top_k(logits, TOP_K)
    top_w = jax.nn.softmax(top_logit, axis=-1)
    n_assign = t * TOP_K
    flat_e = top_e.reshape(-1)
    order = jnp.argsort(flat_e)
    sorted_e = flat_e[order]
    sorted_tok = order // TOP_K
    sorted_w = top_w.reshape(-1)[order]
    counts = jnp.bincount(flat_e, length=N_EXPERTS)
    padded = (counts + MOE_BLOCK - 1) // MOE_BLOCK * MOE_BLOCK
    pad_end = jnp.cumsum(padded)
    pad_start = pad_end - padded
    start = jnp.cumsum(counts) - counts
    dest = pad_start[sorted_e] + jnp.arange(n_assign) - start[sorted_e]
    n_blocks = -(-n_assign // MOE_BLOCK) + N_EXPERTS
    buf_tok = jnp.zeros((n_blocks * MOE_BLOCK,), jnp.int32).at[dest].set(sorted_tok.astype(jnp.int32))
    block_e = jnp.minimum(jnp.searchsorted(pad_end, jnp.arange(n_blocks) * MOE_BLOCK, side='right'),
                          N_EXPERTS - 1)
    xb = h[buf_tok].reshape(n_blocks, MOE_BLOCK, h.shape[-1])

    def expert_block(args):
        xe, e = args
        gate = jnp.minimum(xe @ w_gate[e] + b_gate[e], SWIGLU_LIMIT)
        up = jnp.clip(xe @ w_up[e] + b_up[e], -SWIGLU_LIMIT, SWIGLU_LIMIT)
        act = (up + 1) * (gate * jax.nn.sigmoid(SWIGLU_ALPHA * gate))
        return act @ w_down[e] + b_down[e]

    yb = lax.map(expert_block, (xb, block_e)).reshape(-1, h.shape[-1])
    y = yb[dest] * sorted_w[:, None].astype(h.dtype)
    return jax.ops.segment_sum(y, sorted_tok, num_segments=t)

def first_inputs(seed: int = 0) -> dict:
    key = jax.random.key(seed)
    ks = jax.random.split(key, 32)
    f32 = jnp.float32
    L = DEPTH

    def nrm(k, shape, scale):
        return jax.random.normal(k, shape, f32) * scale

    def gain(k, shape):
        return 1.0 + 0.05 * jax.random.normal(k, shape, f32)

    return {
        "x": nrm(ks[0], (BATCH, SEQ, D_MODEL), 1.0),
        "c": nrm(ks[1], (BATCH, D_MODEL), 1.0),
        "ctx": nrm(ks[2], (BATCH, CTX_LEN, D_MODEL), 1.0),
        "c_ctx": nrm(ks[3], (D_MODEL,), 1.0),
        "w_ada": nrm(ks[4], (L, D_MODEL, N_MOD * D_MODEL), 0.5 * D_MODEL ** -0.5),
        "b_ada": nrm(ks[5], (L, N_MOD * D_MODEL), 0.02),
        "norm_attn": gain(ks[6], (L, D_MODEL)),
        "w_in": nrm(ks[7], (L, D_MODEL, IN_COLS), D_MODEL ** -0.5),
        "q_norm_a": gain(ks[8], (L, HEAD_DIM)),
        "k_norm_a": gain(ks[9], (L, HEAD_DIM)),
        "q_norm_b": gain(ks[10], (L, HEAD_DIM)),
        "k_norm_b": gain(ks[11], (L, HEAD_DIM)),
        "lambda_q1": nrm(ks[12], (L, HEAD_DIM), 0.1),
        "lambda_k1": nrm(ks[13], (L, HEAD_DIM), 0.1),
        "lambda_q2": nrm(ks[14], (L, HEAD_DIM), 0.1),
        "lambda_k2": nrm(ks[15], (L, HEAD_DIM), 0.1),
        "subln_b": gain(ks[16], (L, B_V_DIM)),
        "w_oa": nrm(ks[17], (L, A_WIDTH, D_MODEL), A_WIDTH ** -0.5),
        "w_ob": nrm(ks[18], (L, B_WIDTH, D_MODEL), B_WIDTH ** -0.5),
        "w_out": nrm(ks[19], (L, D_MODEL, D_MODEL), D_MODEL ** -0.5),
        "norm_mlp": gain(ks[20], (L, D_MODEL)),
        "router_w": nrm(ks[21], (L, D_MODEL, N_EXPERTS), D_MODEL ** -0.5),
        "router_b": nrm(ks[22], (L, N_EXPERTS), 0.01),
        "w_gate": nrm(ks[23], (L, N_EXPERTS, D_MODEL, D_EXPERT), D_MODEL ** -0.5),
        "b_gate": nrm(ks[24], (L, N_EXPERTS, D_EXPERT), 0.02),
        "w_up": nrm(ks[25], (L, N_EXPERTS, D_MODEL, D_EXPERT), D_MODEL ** -0.5),
        "b_up": nrm(ks[26], (L, N_EXPERTS, D_EXPERT), 0.02),
        "w_down": nrm(ks[27], (L, N_EXPERTS, D_EXPERT, D_MODEL), D_EXPERT ** -0.5),
        "b_down": nrm(ks[28], (L, N_EXPERTS, D_MODEL), 0.02),
    }

def first_block(x, c, ctx, c_ctx, w_ada, b_ada, norm_attn, w_in, q_norm_a, k_norm_a, q_norm_b,
              k_norm_b, lambda_q1, lambda_k1, lambda_q2, lambda_k2, subln_b, w_oa, w_ob, w_out,
              norm_mlp, router_w, router_b, w_gate, b_gate, w_up, b_up, w_down, b_down):
    b, s, d = x.shape
    rows = s // GRID_W
    cos, sin = _axial_rope(rows)
    cx = ctx
    for l in range(DEPTH):
        last = l == DEPTH - 1
        lam_init = 0.8 - 0.6 * math.exp(-0.3 * l)
        lam = (jnp.exp(jnp.sum(lambda_q1[l].astype(jnp.float32) * lambda_k1[l].astype(jnp.float32)))
               - jnp.exp(jnp.sum(lambda_q2[l].astype(jnp.float32) * lambda_k2[l].astype(jnp.float32)))
               + lam_init)
        mod_x = (jax.nn.silu(c) @ w_ada[l] + b_ada[l])[:, None, :]
        mod_c = (jax.nn.silu(c_ctx) @ w_ada[l] + b_ada[l])[None, None, :]
        sh_a, sc_a, g_a, sh_m, sc_m, g_m = jnp.split(mod_x, N_MOD, axis=-1)
        csh_a, csc_a, cg_a, csh_m, csc_m, cg_m = jnp.split(mod_c, N_MOD, axis=-1)
        proj = functools.partial(_project, w_in=w_in[l], q_norm_a=q_norm_a[l], k_norm_a=k_norm_a[l],
                                 q_norm_b=q_norm_b[l], k_norm_b=k_norm_b[l])

        hx = _modulate(_rmsnorm(x, norm_attn[l]), sh_a, sc_a)
        hc = _modulate(_rmsnorm(cx, norm_attn[l]), csh_a, csc_a)
        qa, ka, va, qb, kb, vb, ga, gb = proj(hx)
        cqa, cka, cva, cqb, ckb, cvb, cga, cgb = proj(hc)
        qa, ka = _apply_rope(qa, cos, sin), _apply_rope(ka, cos, sin)
        qb, kb = _apply_rope(qb, cos, sin), _apply_rope(kb, cos, sin)
        ka_all = jnp.concatenate([ka, cka], axis=1)
        va_all = jnp.concatenate([va, cva], axis=1)
        kb_all = jnp.concatenate([kb, ckb], axis=1)
        vb_all = jnp.concatenate([vb, cvb], axis=1)
        ya = _sweep_query_blocks(_gqa_attend, qa, ka_all, va_all)
        yb = _sweep_query_blocks(lambda qq, kk, vv: _diff_attend(qq, kk, vv, lam), qb, kb_all, vb_all)
        yb = _diff_out(yb, subln_b[l], lam_init)
        x = x + g_a * _merge(ya, yb, ga, gb, w_oa[l], w_ob[l], w_out[l])
        if not last:
            cya = _gqa_attend(cqa, cka, cva)
            cyb = _diff_out(_diff_attend(cqb, ckb, cvb, lam), subln_b[l], lam_init)
            cx = cx + cg_a * _merge(cya, cyb, cga, cgb, w_oa[l], w_ob[l], w_out[l])

        moe = functools.partial(_moe, router_w=router_w[l], router_b=router_b[l], w_gate=w_gate[l],
                                b_gate=b_gate[l], w_up=w_up[l], b_up=b_up[l], w_down=w_down[l],
                                b_down=b_down[l])
        hx = _modulate(_rmsnorm(x, norm_mlp[l]), sh_m, sc_m)
        x = x + g_m * moe(hx.reshape(b * s, d)).reshape(b, s, d)
        if not last:
            hc = _modulate(_rmsnorm(cx, norm_mlp[l]), csh_m, csc_m)
            cx = cx + cg_m * moe(hc.reshape(-1, d)).reshape(cx.shape)
    return x


N_HEADS_SB = 8
N_HEADS_FOX = 8
N_HEADS_MOBA = 8
BRANCH_WIDTH = 8 * HEAD_DIM
N_BRANCH_2 = 3
D_FF = 4 * D_MODEL
MOBA_BLOCK = 256
MOBA_TOPK = 3
MOBA_Q_CHUNK = 32
RMS_EPS = 1e-6
NEG_INF = -1e30
FORGET_BIAS_INIT = 2.0
IN_COLS_2 = 9 * BRANCH_WIDTH + N_HEADS_FOX + N_BRANCH_2 * D_MODEL


def rmsnorm(x, g):
    xf = x.astype(jnp.float32)
    y = xf * lax.rsqrt(jnp.mean(xf * xf, axis=-1, keepdims=True) + RMS_EPS)
    return (y * g.astype(jnp.float32)).astype(x.dtype)

def split_in_proj(proj):
    sizes = [BRANCH_WIDTH] * 6 + [N_HEADS_FOX] + [BRANCH_WIDTH] * 3 + [N_BRANCH_2 * D_MODEL]
    points = [int(p) for p in np.cumsum(sizes)[:-1]]
    return jnp.split(proj, points, axis=-1)

def to_heads(t, n_heads):
    B, S, _ = t.shape
    return t.reshape(B, S, n_heads, HEAD_DIM).transpose(0, 2, 1, 3)

def merge_heads(t):
    B, H, S, d = t.shape
    return t.transpose(0, 2, 1, 3).reshape(B, S, H * d)

def alibi_slopes(n):
    return 2.0 ** (-8.0 * jnp.arange(1, n + 1, dtype=jnp.float32) / n)

def stick_breaking_attention(q, k, v):
    B, H, S, d = q.shape
    scale = 1.0 / math.sqrt(d)
    kf = k.astype(jnp.float32)
    vf = v.astype(jnp.float32)
    key_pos = jnp.arange(S)

    def block(i):
        t0 = i * Q_BLOCK
        qb = lax.dynamic_slice_in_dim(q, t0, Q_BLOCK, axis=2).astype(jnp.float32)
        z = jnp.einsum('bhqd,bhkd->bhqk', qb, kf) * scale
        q_pos = t0 + jnp.arange(Q_BLOCK)
        past = key_pos[None, :] < q_pos[:, None]
        log_1m = jnp.where(past, -jax.nn.softplus(z), 0.0)
        tail = lax.cumsum(log_1m, axis=3, reverse=True) - log_1m
        w = jnp.where(past, jnp.exp(jax.nn.log_sigmoid(z) + tail), 0.0)
        return jnp.einsum('bhqk,bhkd->bhqd', w, vf)

    out = lax.map(block, jnp.arange(S // Q_BLOCK))
    out = out.transpose(1, 2, 0, 3, 4).reshape(B, H, S, d)
    return out.astype(q.dtype)

def forgetting_attention(q, k, v, f_logit):
    B, H, S, d = q.shape
    scale = 1.0 / math.sqrt(d)
    kf = k.astype(jnp.float32)
    vf = v.astype(jnp.float32)
    c = lax.cumsum(jax.nn.log_sigmoid(f_logit.astype(jnp.float32)), axis=2)
    key_pos = jnp.arange(S)

    def block(i):
        t0 = i * Q_BLOCK
        qb = lax.dynamic_slice_in_dim(q, t0, Q_BLOCK, axis=2).astype(jnp.float32)
        cq = lax.dynamic_slice_in_dim(c, t0, Q_BLOCK, axis=2)
        logits = jnp.einsum('bhqd,bhkd->bhqk', qb, kf) * scale + (cq[..., :, None] - c[..., None, :])
        q_pos = t0 + jnp.arange(Q_BLOCK)
        causal = key_pos[None, :] <= q_pos[:, None]
        p = jax.nn.softmax(jnp.where(causal, logits, NEG_INF), axis=-1)
        return jnp.einsum('bhqk,bhkd->bhqd', p, vf)

    out = lax.map(block, jnp.arange(S // Q_BLOCK))
    out = out.transpose(1, 2, 0, 3, 4).reshape(B, H, S, d)
    return out.astype(q.dtype)

def moba_attention(q, k, v, slopes):
    B, H, S, d = q.shape
    scale = 1.0 / math.sqrt(d)
    n_kb = -(-S // MOBA_BLOCK)
    n_top = min(MOBA_TOPK, n_kb)
    pad = n_kb * MOBA_BLOCK - S
    kf = jnp.pad(k.astype(jnp.float32), ((0, 0), (0, 0), (0, pad), (0, 0)))
    vf = jnp.pad(v.astype(jnp.float32), ((0, 0), (0, 0), (0, pad), (0, 0)))
    k_blocks = kf.reshape(B, H, n_kb, MOBA_BLOCK, d)
    v_blocks = vf.reshape(B, H, n_kb, MOBA_BLOCK, d)
    k_mean = jnp.mean(k_blocks, axis=3)
    b_idx = jnp.arange(B)[:, None, None, None]
    h_idx = jnp.arange(H)[None, :, None, None]
    blk_ids = jnp.arange(n_kb)
    offs = jnp.arange(MOBA_BLOCK)
    slope = slopes[None, :, None, None]
    n_sel = n_top * MOBA_BLOCK

    def chunk(c):
        t0 = c * MOBA_Q_CHUNK
        own = t0 // MOBA_BLOCK
        qc = lax.dynamic_slice_in_dim(q, t0, MOBA_Q_CHUNK, axis=2).astype(jnp.float32)
        q_pos = t0 + jnp.arange(MOBA_Q_CHUNK)
        route = jnp.einsum('bhqd,bhnd->bhqn', qc, k_mean)
        route = jnp.where(blk_ids < own, route, NEG_INF)
        _, sel = lax.top_k(route, n_top)
        sel_valid = sel < own
        k_sel = k_blocks[b_idx, h_idx, sel]
        v_sel = v_blocks[b_idx, h_idx, sel]
        s_sel = jnp.einsum('bhqd,bhqrnd->bhqrn', qc, k_sel) * scale
        pos_sel = sel[..., None] * MOBA_BLOCK + offs
        s_sel = s_sel - slope[..., None] * (q_pos[:, None, None] - pos_sel)
        s_sel = jnp.where(sel_valid[..., None], s_sel, NEG_INF).reshape(B, H, MOBA_Q_CHUNK, n_sel)
        k_own = lax.dynamic_slice_in_dim(kf, own * MOBA_BLOCK, MOBA_BLOCK, axis=2)
        v_own = lax.dynamic_slice_in_dim(vf, own * MOBA_BLOCK, MOBA_BLOCK, axis=2)
        rel = q_pos[:, None] - (own * MOBA_BLOCK + offs)[None, :]
        s_own = jnp.einsum('bhqd,bhnd->bhqn', qc, k_own) * scale - slope * rel
        s_own = jnp.where(rel >= 0, s_own, NEG_INF)
        p = jax.nn.softmax(jnp.concatenate([s_sel, s_own], axis=-1), axis=-1)
        p_sel = p[..., :n_sel].reshape(B, H, MOBA_Q_CHUNK, n_top, MOBA_BLOCK)
        p_own = p[..., n_sel:]
        return (jnp.einsum('bhqrn,bhqrnd->bhqd', p_sel, v_sel)
                + jnp.einsum('bhqn,bhnd->bhqd', p_own, v_own))

    out = lax.map(chunk, jnp.arange(S // MOBA_Q_CHUNK))
    out = out.transpose(1, 2, 0, 3, 4).reshape(B, H, S, d)
    return out.astype(q.dtype)

def second_inputs(seed: int = 0) -> dict:
    key = jax.random.key(seed)
    ks = jax.random.split(key, 11)
    f32 = jnp.float32
    x = jax.random.normal(ks[0], (BATCH, SEQ, D_MODEL), f32)
    norm_mix = 1.0 + 0.02 * jax.random.normal(ks[1], (DEPTH, D_MODEL), f32)
    w_in = jax.random.normal(ks[2], (DEPTH, D_MODEL, IN_COLS_2), f32) * D_MODEL ** -0.5
    b_forget = FORGET_BIAS_INIT + 0.5 * jax.random.normal(ks[3], (DEPTH, N_HEADS_FOX), f32)
    w_branch = jax.random.normal(ks[4], (DEPTH, N_BRANCH_2, BRANCH_WIDTH, D_MODEL), f32) * BRANCH_WIDTH ** -0.5
    w_out = jax.random.normal(ks[5], (DEPTH, D_MODEL, D_MODEL), f32) * D_MODEL ** -0.5
    norm_mlp = 1.0 + 0.02 * jax.random.normal(ks[6], (DEPTH, D_MODEL), f32)
    w_up = jax.random.normal(ks[7], (DEPTH, D_MODEL, D_FF), f32) * D_MODEL ** -0.5
    w_down = jax.random.normal(ks[8], (DEPTH, D_FF, D_MODEL), f32) * D_FF ** -0.5
    norm_final = 1.0 + 0.02 * jax.random.normal(ks[9], (D_MODEL,), f32)
    return {"x": x, "norm_mix": norm_mix, "w_in": w_in, "b_forget": b_forget,
            "w_branch": w_branch, "w_out": w_out, "norm_mlp": norm_mlp,
            "w_up": w_up, "w_down": w_down, "norm_final": norm_final}

def second_block(x, norm_mix, w_in, b_forget, w_branch, w_out, norm_mlp, w_up, w_down, norm_final):
    B, S, _ = x.shape
    slopes = alibi_slopes(N_HEADS_MOBA)
    for l in range(DEPTH):
        h = rmsnorm(x, norm_mix[l])
        proj = jnp.einsum('bsd,de->bse', h, w_in[l])
        q_a, k_a, v_a, q_b, k_b, v_b, f_b, q_c, k_c, v_c, g = split_in_proj(proj)
        o_a = stick_breaking_attention(to_heads(q_a, N_HEADS_SB), to_heads(k_a, N_HEADS_SB),
                                       to_heads(v_a, N_HEADS_SB))
        f_logit = (f_b + b_forget[l]).transpose(0, 2, 1)
        o_b = forgetting_attention(to_heads(q_b, N_HEADS_FOX), to_heads(k_b, N_HEADS_FOX),
                                   to_heads(v_b, N_HEADS_FOX), f_logit)
        o_c = moba_attention(to_heads(q_c, N_HEADS_MOBA), to_heads(k_c, N_HEADS_MOBA),
                             to_heads(v_c, N_HEADS_MOBA), slopes)
        branches = jnp.stack([merge_heads(o_a), merge_heads(o_b), merge_heads(o_c)], axis=2)
        lifted = jnp.einsum('bsnw,nwd->bsnd', branches, w_branch[l])
        gates = jax.nn.sigmoid(g.reshape(B, S, N_BRANCH_2, D_MODEL))
        mixed = jnp.sum(gates * lifted, axis=2)
        x = x + jnp.einsum('bsd,de->bse', mixed, w_out[l])
        h = rmsnorm(x, norm_mlp[l])
        hid = jnp.square(jax.nn.relu(jnp.einsum('bsd,df->bsf', h, w_up[l])))
        x = x + jnp.einsum('bsf,fd->bsd', hid, w_down[l])
    return rmsnorm(x, norm_final)


def setup_inputs(seed=0):
    out = dict(first_inputs(seed))
    for name, value in second_inputs(seed + 1).items():
        if name != "x":
            out[name + "_2"] = value
    return out


def reference(
    x, c, ctx, c_ctx, w_ada, b_ada, norm_attn, w_in, q_norm_a, k_norm_a, q_norm_b, k_norm_b,
    lambda_q1, lambda_k1, lambda_q2, lambda_k2, subln_b, w_oa, w_ob, w_out, norm_mlp, router_w,
    router_b, w_gate, b_gate, w_up, b_up, w_down, b_down, norm_mix_2, w_in_2, b_forget_2,
    w_branch_2, w_out_2, norm_mlp_2, w_up_2, w_down_2, norm_final_2,
):
    x = first_block(
        x, c, ctx, c_ctx, w_ada, b_ada, norm_attn, w_in, q_norm_a, k_norm_a, q_norm_b, k_norm_b,
        lambda_q1, lambda_k1, lambda_q2, lambda_k2, subln_b, w_oa, w_ob, w_out, norm_mlp,
        router_w, router_b, w_gate, b_gate, w_up, b_up, w_down, b_down,
    )
    return second_block(
        x, norm_mix_2, w_in_2, b_forget_2, w_branch_2, w_out_2, norm_mlp_2, w_up_2, w_down_2,
        norm_final_2,
    )


_drawn_inputs = setup_inputs


def setup_inputs(seed=0):
    import zlib

    import numpy as np

    out = dict(_drawn_inputs(seed))
    spreads = {}
    factors = {'norm_attn': 4.557,
     'q_norm_a': 8.0,
     'k_norm_a': 8.0,
     'q_norm_b': 6.902,
     'k_norm_b': 7.443,
     'lambda_q1': 4.374,
     'lambda_q2': 181.104,
     'lambda_k2': 4.676,
     'subln_b': 3.871,
     'router_b': 3.994,
     'b_gate': 8.0,
     'b_up': 8.0,
     'b_down': 8.0,
     'norm_mix_2': 4.473,
     'norm_mlp_2': 9.299,
     'norm_final_2': 19.997}
    for name, (base, spread) in spreads.items():
        noise = np.random.default_rng([zlib.crc32(name.encode()), seed]).standard_normal(out[name].shape)
        drawn = base * np.exp(spread * noise) if base else spread * noise
        out[name] = __import__('jax').numpy.asarray(drawn.astype(out[name].dtype))
    for name, factor in factors.items():
        out[name] = (out[name] * factor).astype(out[name].dtype)
    return out
```

```python
import math
from contextlib import ExitStack

import numpy as np

import concourse.bass as bass
from concourse import mybir

F32 = mybir.dt.float32
I32 = mybir.dt.int32
ALU = mybir.AluOpType
ACT = mybir.ActivationFunctionType
AX = mybir.AxisListType

P = 128
T = 256
TT = T // P
CTX = 256
D = 1024
KC = D // P
HD = 64
A_HEADS, A_KV, B_HEADS = 8, 2, 4
EPS, SUBLN_EPS = 1e-6, 1e-5
LAM_INIT = 0.8 - 0.6 * math.exp(-0.0)
N_EXP, TOP_K = 32, 4
LIMIT, ALPHA = 7.0, 1.702
GRID_W, ROPE_THETA = 64, 10000.0
NEG = -1e30
FFN_COLS = 4096
HEADS2 = 8

SLOT = 4096
RING = 6
CAP = 64
EG = 4
GROUPS = N_EXP // EG
BLK_EXP = 6
EPAD = N_EXP + EG

W_ADA1, W_KVA, W_KB, W_VB, W_QA, W_QB, W_GATE = 0, 4, 5, 6, 7, 8, 9
W_ADA2, W_OA, W_OB, W_OUT, W_MOE = 13, 21, 22, 23, 25
W_QKV2 = W_MOE + N_EXP * BLK_EXP
W_GB2 = W_QKV2 + 9
W_BR2 = W_GB2 + 6
W_OUT2 = W_BR2 + 3
W_UP2 = W_OUT2 + 2
W_DOWN2 = W_UP2 + 8
W_END = W_DOWN2 + 8

C_ID, C_SUF, C_STRICT, C_ULE, C_ONES, C_ADDT, C_ZERO, C_CMASK, C_NREL = (
    0, 128, 256, 384, 512, 640, 768, 896, 1024)
C_ROPEC, C_ROPES, C_IOTA, C_ROW0 = 1280, 1408, 1536, 1600
N_CONST = 1601

V_C, V_BADA, V_NA, V_NM, V_NX2, V_NM2, V_SUB = 0, 16, 64, 72, 80, 88, 96
N_VEC = 97
R_GAIN, R_LAM, R_RB, R_FB = 0, 256, 512, 544
N_ROW = 552


def constants():
    c = np.zeros((P, N_CONST), np.float32)
    i = np.arange(P)
    c[:, C_ID:C_ID + P] = np.eye(P)
    c[:, C_SUF:C_SUF + P] = i[:, None] >= i[None, :]
    c[:, C_STRICT:C_STRICT + P] = i[:, None] < i[None, :]
    c[:, C_ULE:C_ULE + P] = i[:, None] <= i[None, :]
    c[:, C_ONES:C_ONES + P] = 1.0
    c[:, C_ADDT:C_ADDT + P] = np.where(i[:, None] < i[None, :], 0.0, NEG)
    c[:, C_CMASK:C_CMASK + P] = np.where(i[None, :] <= i[:, None], 0.0, NEG)
    c[:, C_NREL:C_NREL + T] = np.arange(T)[None, :] - P - i[:, None]
    pairs = HD // 4
    inv = (1.0 / (ROPE_THETA ** (np.arange(pairs, dtype=np.float32) / pairs))).astype(np.float32)
    tok = np.arange(T)
    ang = np.concatenate([(tok // GRID_W).astype(np.float32)[:, None] * inv,
                          (tok % GRID_W).astype(np.float32)[:, None] * inv], axis=-1)
    cos, sin = np.cos(ang), np.sin(ang)
    both = np.repeat(cos, 2, axis=1)
    signed = np.stack([-sin, sin], axis=-1).reshape(T, HD)
    for t in range(TT):
        c[:, C_ROPEC + HD * t:C_ROPEC + HD * (t + 1)] = both[P * t:P * (t + 1)]
        c[:, C_ROPES + HD * t:C_ROPES + HD * (t + 1)] = signed[P * t:P * (t + 1)]
    c[:, C_IOTA:C_IOTA + CAP] = np.arange(CAP)[None, :]
    c[::32, C_ROW0] = 1.0
    return c


def two_blocks(nc, t, out):
    ctx = ExitStack()
    with ctx:
        def sb(name, words, dt=F32):
            return ctx.enter_context(nc.sbuf_tensor(name, [P, words], dt))

        sems = {}

        def sem(name):
            if name not in sems:
                sems[name] = ctx.enter_context(nc.semaphore(name))
            return sems[name]

        ring = sb("ring", RING * SLOT)
        const = sb("const", N_CONST)
        vec = sb("vec", N_VEC)
        row = sb("row", N_ROW)
        xres_t = sb("xres", TT * D)
        g_attn = sb("g_attn", D)
        g_moe = sb("g_moe", D)
        rw_t = sb("router_weights", KC * N_EXP)
        wf_t = sb("forget_weights", KC * HEADS2)
        stat = sb("stat", 256)
        npass_t = sb("npass", 1, I32)
        ARENA = 21504
        arena = sb("arena", ARENA)
        ps_t = ctx.enter_context(nc.psum_tensor("ps", [P, 8 * 512], F32))

        def area(at, words):
            assert at + words <= ARENA
            return arena[:, at:at + words]

        def bank(b, n=512):
            return ps_t[:, 512 * b:512 * b + n]

        def cst(at, n=P):
            return const[:, at:at + n]

        def slot(i):
            s = i % RING
            return ring[:, s * SLOT:(s + 1) * SLOT]

        ident = cst(C_ID)
        xres = xres_t[:, :].rearrange("p (t d) -> p t d", t=TT)
        rw = rw_t[:, :].rearrange("p (j e) -> p j e", j=KC)
        wf = wf_t[:, :].rearrange("p (j e) -> p j e", j=KC)

        hT = area(0, 4096).rearrange("p (j q) -> p j q", j=KC)
        PTA = area(0, 4096).rearrange("p (s k q) -> p s k q", s=4, k=4)
        PTB = area(0, 2048).rearrange("p (s k q) -> p s k q", s=4, k=4)
        QA = area(4096, 2048).rearrange("p (h q) -> p h q", h=8)
        QB = area(6144, 2048).rearrange("p (h q) -> p h q", h=8)
        KTA = area(8192, 512)
        KTB = area(8704, 2048).rearrange("p (h k) -> p h k", h=4)
        VA = area(10752, 512).rearrange("p (i c) -> p i c", i=4)
        VB = area(11264, 2048).rearrange("p (i c) -> p i c", i=4)
        sig = area(13312, 4096).rearrange("p (s w) -> p s w", s=8)
        xn4 = area(13312, 4096).rearrange("p (i d) -> p i d", i=4)
        ctx_in = area(17408, 2048).rearrange("p (i d) -> p i d", i=2)
        raw = area(17408, 1024).rearrange("p (b w) -> p b w", b=2)
        sq = area(18432, 1024).rearrange("p (b w) -> p b w", b=2)
        prob = area(17408, 2048).rearrange("p (b w) -> p b w", b=4)
        modp = area(19456, 1024).rearrange("p (b w) -> p b w", b=2)
        rt1, rt2 = area(19456, 512), area(19968, 512)
        hat = area(20480, 1024).rearrange("p (b w) -> p b w", b=2)
        yaT = area(19456, 1024).rearrange("p (c q) -> p c q", c=4)
        ybT = area(20480, 1024).rearrange("p (c q) -> p c q", c=4)
        onorm = area(4096, 256).rearrange("p (b w) -> p b w", b=2)
        squares = area(4352, 256).rearrange("p (b w) -> p b w", b=2)
        mergedT = area(8704, 2048).rearrange("p (j q) -> p j q", j=KC)
        mtmp = area(4096, 1024).rearrange("p (b w) -> p b w", b=2)
        cs_t = rw_t[:, :].rearrange("p (j m) -> p j m", j=KC)

        ss = stat[:, 0:8]
        rstd = stat[:, 8:16]
        sigc = stat[:, 16:32]
        lam2 = stat[:, 32:34]
        lam = stat[:, 34:35]
        sub08 = stat[:, 35:36]
        nh_ss = stat[:, 36:44]
        nh_rs = stat[:, 44:52]
        modT = ctx.enter_context(nc.sbuf_tensor("modT", [P, 48, 2], F32))
        scale_a = ctx.enter_context(nc.sbuf_tensor("scale_a", [P, KC, 2], F32))
        scale_m = ctx.enter_context(nc.sbuf_tensor("scale_m", [P, KC], F32))
        nmax = stat[:, 64:96]
        lsum = stat[:, 96:128]
        linv = stat[:, 128:160]
        bss = stat[:, 160:168]
        brs = stat[:, 168:176]

        b_all = area(0, 1024)
        hperm = area(1024, 2048).rearrange("p (t h c d) -> p t h c d", t=TT, h=2, c=4)
        xn2 = area(3072, 2048).rearrange("p (t d) -> p t d", t=TT)
        xeT = area(3072, 2048).rearrange("p (j s) -> p j s", j=KC)
        hmT = area(5120, 2048).rearrange("p (j q) -> p j q", j=KC)
        acc = area(7168, 2048).rearrange("p (t d) -> p t d", t=TT)
        S4 = area(9216, 512).rearrange("p (t e s) -> p t e s", t=TT, e=EG)
        WS4 = area(9728, 512).rearrange("p (t e s) -> p t e s", t=TT, e=EG)
        WST = area(10240, 512)
        gbuf, ubuf, sbuf_, tbuf = (area(10752 + 512 * i, 512) for i in range(4))
        abuf = area(12800, 512)
        actT = area(13312, 512).rearrange("p (c f s) -> p c f s", c=4, f=2)
        ypair = area(13824, 1024)
        esel = area(14848, 3 * EG * CAP).rearrange("p (m e s) -> p m e s", m=3, e=EG)
        o = 14848 + 3 * EG * CAP
        logit = area(o, TT * EPAD).rearrange("p (t e) -> p t e", t=TT)
        lrep = area(o + 80, TT * EPAD).rearrange("p (t e) -> p t e", t=TT)
        rtab = area(o + 160, TT * EPAD).rearrange("p (t e) -> p t e", t=TT)
        wtab = area(o + 240, TT * EPAD).rearrange("p (t e) -> p t e", t=TT)
        emask = area(o + 320, TT * N_EXP).rearrange("p (t e) -> p t e", t=TT)
        eexp = area(o + 400, TT * N_EXP).rearrange("p (t e) -> p t e", t=TT)
        top8 = area(o + 480, TT * 8).rearrange("p (t e) -> p t e", t=TT)
        esm = area(o + 500, 16)

        hT2 = area(0, 2048).rearrange("p (j q) -> p j q", j=KC)
        Q2 = area(2048, 6144).rearrange("p (b h q) -> p b h q", b=3, h=8)
        K2 = area(8192, 3072).rearrange("p (b c k) -> p b c k", b=3, c=4)
        V2 = area(11264, 3072).rearrange("p (b t c) -> p b t c", b=3, t=TT)
        OT = area(14336, 3072).rearrange("p (b c q) -> p b c q", b=3, c=4)
        xn3 = area(17408, 2048).rearrange("p (t d) -> p t d", t=TT)
        zs, te, ln1, sp, sw = (area(17408 + 768 * i, 768) for i in range(5))
        CM = area(17408, 768).rearrange("p (b w) -> p b w", b=2)
        P2 = area(18176, 768).rearrange("p (b w) -> p b w", b=2)
        PT2 = area(18944, 1536).rearrange("p (b w) -> p b w", b=4)
        fsm = area(21248, 128)
        sig2 = area(2048, 4096).rearrange("p (n s w) -> p n s w", n=2, s=4)
        mixT = area(8192, 2048).rearrange("p (j q) -> p j q", j=KC)
        mt2 = area(11264, 512)
        hid = area(6656, 8192).rearrange("p (j q) -> p j q", j=32)
        relu = area(14848, 1024).rearrange("p (b w) -> p b w", b=2)
        yout = area(17408, 2048).rearrange("p (t d) -> p t d", t=TT)

        STICK_STEPS = 6
        TURN_STEP = 14

        def step_bank(s):
            return s % 4 if s < STICK_STEPS else s % 2 if s < 28 else s - 26

        def filler_step(u):
            return TURN_STEP + u - u // 8 if u < 16 and u % 8 < 7 else None

        block_used = sem("block_used")
        loaded = [sem(f"block_loaded{s}") for s in range(RING)]

        X1 = {n: sem("x_" + n) for n in (
            "gate_done", "up_done", "gate_read", "up_read", "sig_done", "act_done", "tr_done", "tr_read",
            "down_done", "y_read", "comb_done", "comb_read", "s4_ready", "ws4_ready", "sel_ready",
            "gather_done", "gather_read")}
        X2 = dict(X1)
        X1["free"], X1["loaded"] = block_used, loaded
        X2["free"] = sem("more_block_used")
        X2["loaded"] = [sem(f"more_block_loaded{i}") for i in range(RING)]

        block = ctx.enter_context(nc.Block())

        def wq_view(i, cols=512):
            return slot(i)[:, 0:KC * cols].rearrange("p (j n) -> p j n", j=KC)

        def w4_view(i):
            return slot(i).rearrange("p (c n) -> p c n", c=4)

        def ov_passes(e, body, before=None):
            n = e.value_load(npass_t[0:1, 0:1], min_val=1, max_val=T // CAP)
            with e.If(n > 1):
                if before:
                    before()
                with e.Fori(1, n) as p:
                    e.drain()
                    e.sem_inc(sem("x2_enter"), 1)
                    e.wait_ge(sem("x2_enter"), p * 5)
                    e.sem_inc(sem("x2_entered"), 1)
                    body(p)
                    e.drain()
                    e.sem_inc(sem("x2_leave"), 1)
                    e.wait_ge(sem("x2_leave"), p * 5)
                    e.sem_inc(sem("x2_left"), 1)

        @block.sync
        def _(sp_):
            def load(i, dst, src):
                if i >= RING:
                    sp_.wait_ge(block_used, i - RING + 1)
                sp_.dma_start(dst, src).then_inc(loaded[i % RING], 16)

            def load_cols(i, w, c0, cols=512):
                load(i, wq_view(i, cols), w[:, c0:c0 + cols].rearrange("(j p) n -> p j n", p=P))

            def load_rows(i, w):
                load(i, w4_view(i), w.rearrange("(c p) n -> p c n", p=P))

            for i in range(4):
                load_cols(W_ADA1 + i, t["w_ada"], 512 * i)
            w_in = t["w_in"]
            load_cols(W_KVA, w_in, 512, 256)
            for i, c0 in ((W_KB, 1280), (W_VB, 1792), (W_QA, 0), (W_QB, 768)):
                load_cols(i, w_in, c0)
            for i in range(4):
                load_cols(W_GATE + i, w_in, 2304 + 512 * i)
            for i in range(8):
                load_cols(W_ADA2 + i, t["w_ada"], 2048 + 512 * i)
            load_rows(W_OA, t["w_oa"])
            load_rows(W_OB, t["w_ob"])
            for i in range(2):
                load_cols(W_OUT + i, t["w_out"], 512 * i)

            def expert_loads(X, it, g, first_block, free):
                for q in range(EG):
                    for m, name in enumerate(("w_gate", "w_up", "w_down")):
                        for half in range(2):
                            k = q * BLK_EXP + m * 2 + half
                            i = first_block + k
                            sp_.wait_ge(X["free"], it * (EG * BLK_EXP) + (free + k))
                            src = t[name][bass.ds(g * EG + q, 1), half * 512:half * 512 + 512, :]
                            sp_.dma_start(slot(i), src.rearrange("e (p c) n -> p (e c n)", c=4)
                                          ).then_inc(X["loaded"][i % RING], 16)

            with sp_.Fori(0, GROUPS) as it:
                expert_loads(X1, it, it, W_MOE, W_MOE - RING + 1)
            sp_.wait_ge(sem("npass_ready"), 1)

            def more_loads(p):
                with sp_.Fori(0, GROUPS) as g:
                    expert_loads(X2, (p - 1) * GROUPS + g, g, 0, 1)
            ov_passes(sp_, more_loads)

            w_in2 = t["w_in_2"]
            for i, c0 in enumerate((0, 512, 1024, 1536, 2048, 2560, 3080, 3592, 4104)):
                load_cols(W_QKV2 + i, w_in2, c0)
            for i in range(6):
                load_cols(W_GB2 + i, w_in2, 4616 + 512 * i)
            for n in range(3):
                load_rows(W_BR2 + n, t["w_branch_2"][n])
            for i in range(2):
                load_cols(W_OUT2 + i, t["w_out_2"], 512 * i)
            for i in range(8):
                load_cols(W_UP2 + i, t["w_up_2"], 512 * i)
            for i in range(8):
                load_rows(W_DOWN2 + i, t["w_down_2"][512 * i:512 * i + 512, :])
            for tt in range(TT):
                sp_.wait_ge(sem("y_done"), tt + 1)
                sp_.dma_start(out[P * tt:P * tt + P, :], yout[:, tt, :]).then_inc(sem("stored"), 16)
            sp_.wait_ge(sem("stored"), 16 * TT)

        @block.gpsimd
        def _(pool):
            pool.memset(area(4096, 4096), 0.0).then_inc(sem("q_zeroed"), 1)
            pool.memset(stat[:, 240:248], -0.5)
            pool.drain()
            roots = [0]

            def inverse_root(a):
                roots[0] += 1
                pool.wait_ge(sem("mean_ready"), roots[0])
                pool.tensor_tensor(a, a, stat[:, 240:240 + a.shape[1]], ALU.pow).then_inc(sem("root_done"), 1)

            inverse_root(rstd[:, 0:4])
            for u in range(12):
                inverse_root(nh_rs[:, 0:2 if u < 4 else 8])
            for i in range(8):
                inverse_root(brs[:, i:i + 1])
            inverse_root(rstd[:, 0:2])
            pool.wait_ge(sem("x1_done"), 4)
            pool.memset(acc, 0.0).then_inc(sem("acc_zeroed"), 1)
            pool.wait_ge(sem("npass_ready"), 1)
            ov_passes(pool, lambda p: None)
            inverse_root(rstd[:, 0:2])
            pool.wait_ge(sem("x2_done"), 2)
            for b in range(3):
                pool.memset(Q2[:, b], 0.0).then_inc(sem("q2_zeroed"), 1)
            for _ in range(2):
                inverse_root(rstd[:, 0:2])

        @block.scalar
        def _(act):
            act.dma_start(vec[:, :], t["vec"]).then_inc(sem("vec_in"), 16)
            for i in range(TT):
                act.dma_start(xres[:, i, :], t["x"][P * i:P * i + P, :]).then_inc(sem(f"x_in{i}"), 16)
            for i in range(2):
                act.dma_start(ctx_in[:, i, :], t["ctx"][P * i:P * i + P, :]).then_inc(sem(f"x_in{2 + i}"), 16)
            act.dma_start(const[:, :], t["const"]).then_inc(sem("const_in"), 16)
            act.dma_start(row[:, :], t["row"].broadcast_to([P, N_ROW])).then_inc(sem("row_in"), 16)
            act.dma_start(g_attn[:, :], t["b_ada"][:, 2 * D:3 * D].broadcast_to([P, D])).then_inc(sem("gb_in"), 16)
            act.dma_start(g_moe[:, :], t["b_ada"][:, 5 * D:6 * D].broadcast_to([P, D])).then_inc(sem("gb_in"), 16)
            act.dma_start(wf_t[:, :], t["w_forget"]).then_inc(sem("wf_in"), 16)

            act.wait_ge(sem("vec_in"), 16)
            act.activation(sigc, vec[:, V_C:V_C + 16], ACT.Sigmoid).then_inc(sem("sigc_done"), 1)
            for i in range(4):
                act.wait_ge(sem(f"x_in{i}"), 16)
                src = xres[:, i, :] if i < 2 else ctx_in[:, i - 2, :]
                act.activation(xn4[:, i, :], src, ACT.Square, accum_out=ss[:, i:i + 1]).then_inc(sem("ss_done"), 1)

            def modulation(n):
                act.wait_ge(sem("ada_done"), n + 1)
                if n >= 2:
                    act.wait_ge(sem("modt_done"), n - 1)
                act.activation(modp[:, n % 2, :], bank(n % 2), ACT.Copy).then_inc(sem("modp_done"), 1)

            for n in range(4):
                modulation(n)
            act.wait_ge(sem("mod_ready"), 1)
            for j in range(0, KC, 2):
                act.wait_ge(sem("ht_tr"), j + 1)
                for m in range(2):
                    last = act.activation(hT[:, j, T * m:T * m + T], bank(4 + j % 4)[:, T * m:T * m + T],
                                          ACT.Identity, scale=scale_a[:, j, m:m + 1], bias=modT[:, j, m:m + 1])
                last.then_inc(sem("ht_act"), 1)

            def qk_out(u):
                act.wait_ge(sem("qkt_done"), u + 1)
                b = bank(4 + u % 4).rearrange("p (c q) -> p c q", c=4)
                if u < 4:
                    last = act.activation(KTA[:, P * u:P * u + P], b[:, 0, :], ACT.Copy)
                elif u < 8:
                    last = act.activation(KTB[:, :, P * (u - 4):P * (u - 3)], b, ACT.Copy)
                elif u < 10:
                    if u == 8:
                        act.wait_ge(sem("q_zeroed"), 1)
                    tt = u - 8
                    for g in range(2):
                        for odd in range(2):
                            last = act.activation(
                                QA[64 * g:64 * g + 64, 4 * g + odd:4 * g + 4:2, P * tt:P * tt + P],
                                b[64 * odd:64 * odd + 64, 2 * g:2 * g + 2, :], ACT.Copy, scale=HD ** -0.5)
                else:
                    tt = u - 10
                    for m in range(2):
                        last = act.activation(QB[64 * m:64 * m + 64, m:8:2, P * tt:P * tt + P],
                                              b[64 * m:64 * m + 64, :, :], ACT.Copy, scale=HD ** -0.5)
                last.then_inc(sem("qkt_read"), 1)

            UNIT = [0, 1, 2, 3, 4, 5, 6, 7, None, None, None, None, 8, 9, 10, 11]
            for s in range(24):
                act.wait_ge(sem("proj_done"), s + 1)
                b = bank(s % 4)
                if s < 16 and UNIT[s] is not None:
                    u = UNIT[s]
                    n = P if u < 4 else 512
                    if u >= 2:
                        act.wait_ge(sem("hat_done"), u - 1)
                    act.activation(raw[:, u % 2, 0:n], b[:, 0:n], ACT.Copy)
                    last = act.activation(sq[:, u % 2, 0:n], b[:, 0:n], ACT.Square)
                    if u < 4:
                        last = act.activation(VA[:, u, :], b[:, P:2 * P], ACT.Copy)
                    last.then_inc(sem("proj_read"), 1)
                elif s < 12:
                    act.activation(VB[:, s - 8, :], b, ACT.Copy).then_inc(sem("proj_read"), 1)
                else:
                    act.activation(sig[:, s - 16, :], b, ACT.Sigmoid).then_inc(sem("proj_read"), 1)
                if 3 <= s < 19 and UNIT[s - 3] is not None:
                    qk_out(UNIT[s - 3])
            act.wait_ge(sem("hat_done"), 12)
            for n in range(4, 12):
                modulation(n)
            act.dma_start(rw_t[:, :], t["router_w"]).then_inc(sem("rw_in"), 16)

            act.wait_ge(sem("lam_sums"), 1)
            act.activation(lam2, lam2, ACT.Exp).then_inc(sem("lam_exp"), 1)

            def exps(n):
                act.wait_ge(sem("mx_done"), n + 1)
                if n >= 4:
                    k = n - 4 if n < 20 else 16 + (n - 20) // 2
                    act.wait_ge(sem("pt_done"), k + 1)
                act.activation(prob[:, n % 4, :], bank(n % 3), ACT.Exp, bias=nmax[:, n:n + 1],
                               accum_out=lsum[:, n:n + 1]).then_inc(sem("ex_done"), 1)

            def pt_out(k):
                act.wait_ge(sem("pt_done"), k + 1)
                b = bank(4 + k % 2).rearrange("p (k q) -> p k q", k=4)
                if k < 16:
                    c, hh, qt = k // 4, (k // 2) % 2, k % 2
                    if c >= 2:
                        act.wait_ge(sem("pv_done"), c - 1)
                    dst = PTA[:, 2 * (c % 2) + hh, :, P * qt:P * qt + P]
                else:
                    act.wait_ge(sem("pv_done"), max(3, k - 16 + 1))
                    dst = PTB[:, (k - 16) % 4]
                act.activation(dst, b, ACT.Copy).then_inc(sem("pt_read"), 1)

            def pv_out(v):
                act.wait_ge(sem("pv_done"), v + 1)
                if v < 4:
                    act.activation(yaT[:, v, :], bank(6 + v % 2, T), ACT.Copy).then_inc(sem("ya_read"), 1)
                else:
                    act.drain()
                    act.activation(squares[:, v % 2, :], bank(6 + v % 2, P), ACT.Square,
                                   accum_out=bss[:, v - 4:v - 3]).then_inc(sem("bss_done"), 1)

            def yb_out(i):
                act.wait_ge(sem("ybt_done"), i + 1)
                act.activation(ybT[:, i // 2, P * (i % 2):P * (i % 2) + P], bank(3, P), ACT.Copy,
                               scale=sub08).then_inc(sem("ybt_read"), 1)

            for k in range(24 + 4):
                if k < 16:
                    exps(k)
                elif k < 24:
                    exps(16 + 2 * (k - 16))
                    exps(17 + 2 * (k - 16))
                if 0 <= k - 1 < 24:
                    pt_out(k - 1)
                if k - 2 >= 3 and (k - 2) < 16 and (k - 2) % 4 == 3:
                    pv_out((k - 2) // 4)
                if 16 <= k - 2 < 24:
                    pv_out(4 + k - 2 - 16)
                if 16 <= k - 3 < 24:
                    yb_out(k - 3 - 16)

            act.dma_start(b_all[0:3 * N_EXP, :], t["b_all"]).then_inc(sem("b_all_in"), 16)
            for i in range(TT):
                act.wait_ge(sem("x1_done"), 3 + i)
                act.activation(xn2[:, i, :], xres[:, i, :], ACT.Square,
                               accum_out=ss[:, i:i + 1]).then_inc(sem("ssm_done"), 1)
            for b in range(0, 4, 2):
                act.wait_ge(sem("hm_tr"), b + 1)
                for j in (2 * b, 2 * b + 1):
                    last = act.activation(hmT[:, j, :], bank(4 + b)[:, T * (j % 2):T * (j % 2) + T], ACT.Identity,
                                          scale=scale_m[:, j:j + 1], bias=modT[:, 24 + j, 0:1])
                last.then_inc(sem("hm_act"), 1)
            for i in range(4):
                act.wait_ge(sem("hp_tr"), i + 1)
                act.activation(hperm[:, i // 2, i % 2].rearrange("p c d -> p d c"),
                               bank(4 + i).rearrange("p (d c) -> p d c", c=4), ACT.Copy).then_inc(sem("hp_read"), 1)
            for i in range(TT):
                act.wait_ge(sem("top_done"), i + 1)
                act.activation(eexp[:, i, :], logit[:, i, 0:N_EXP], ACT.Exp,
                               bias=esm[:, i:i + 1]).then_inc(sem("eexp_done"), 1)

            def gather_out(X, n):
                for r in range(4):
                    act.wait_ge(X["gather_done"], n + r + 1)
                    act.activation(xeT[:, 2 * r:2 * r + 2, :],
                                   bank(4 + r % 2).rearrange("p (j s) -> p j s", j=2),
                                   ACT.Copy).then_inc(X["gather_read"], 1)

            def expert_act(X, it, gathers):
                act.wait_ge(X["tr_done"], it * 5 + 1)
                act.activation(WST, bank(3), ACT.Copy).then_inc(X["tr_read"], 1)
                for q in range(EG):
                    act.wait_ge(X["gate_read"], it * EG + (1 + q + 1))
                    act.activation(sbuf_, gbuf, ACT.Sigmoid, scale=ALPHA).then_inc(X["sig_done"], 1)
                    if q == EG - 1:
                        act.wait_ge(X["up_done"], it * EG + EG)
                        gather_out(X, gathers)
                    act.wait_ge(X["tr_done"], it * 5 + (q + 2))
                    act.wait_ge(X["down_done"], it * EG + (1 + q))
                    act.activation(actT, bank(3).rearrange("p (c f s) -> p c f s", c=4, f=2),
                                   ACT.Copy).then_inc(X["tr_read"], 1)
                    act.wait_ge(X["down_done"], it * EG + (1 + q + 1))
                    act.wait_ge(X["comb_done"], it * 8 + (1 if q < 2 else 5))
                    r0 = CAP * (q % 2)
                    act.activation(ypair[r0:r0 + CAP, 0:512], bank(2)[0:CAP, :], ACT.Copy)
                    act.activation(ypair[r0:r0 + CAP, 512:1024], bank(2)[CAP:2 * CAP, :],
                                   ACT.Copy).then_inc(X["y_read"], 1)

            gather_out(X1, 0)
            for name in ("y_read", "tr_read"):
                act.sem_inc(X1[name], 1)
            with act.Fori(0, GROUPS) as it:
                expert_act(X1, it, it * 4 + 4)
            act.wait_ge(sem("npass_ready"), 1)

            def more_act(p):
                gather_out(X2, p * (4 * GROUPS + 4))
                with act.Fori(0, GROUPS) as g:
                    it = p * GROUPS + g
                    expert_act(X2, it, it * 4 + p * 4 + 4)
            ov_passes(act, more_act)

            act.dma_start(g_attn[:, :], t["norm_final"].broadcast_to([P, D])).then_inc(sem("nf_in"), 16)

            def norm_sums(done, name):
                for i in range(TT):
                    act.wait_ge(sem(done), i + 1)
                    act.activation(xn3[:, i, :], xres[:, i, :], ACT.Square,
                                   accum_out=ss[:, i:i + 1]).then_inc(sem(name), 1)

            def norm_out(tag, vcol):
                for b in range(0, 4, 2):
                    act.wait_ge(sem(tag + "_tr"), b + 1)
                    for j in (2 * b, 2 * b + 1):
                        last = act.activation(hT2[:, j, :], bank(4 + b)[:, T * (j % 2):T * (j % 2) + T], ACT.Copy,
                                              scale=vec[:, vcol + j:vcol + j + 1])
                    last.then_inc(sem(tag + "_act"), 1)

            norm_sums("x2_done", "ssx_done")
            norm_out("hx", V_NX2)

            def projected2(s):
                br, kind, half = s // 6, (s // 2) % 3, s % 2
                act.wait_ge(sem("proj2_done"), s + 1)
                b = bank(step_bank(s))
                if s >= 18:
                    n, q = (s - 18) // 4, (s - 18) % 4
                    if q == 0:
                        act.wait_ge(sem("z_done" if n == 0 else "sc2_done"), 4 if n == 0 else 8)
                    last = act.activation(sig2[:, n, q, :], b, ACT.Copy)
                elif kind == 0:
                    if half == 0:
                        act.wait_ge(sem("q2_zeroed"), br + 1)
                    for odd in range(2):
                        last = act.activation(
                            Q2[64 * odd:64 * odd + 64, br, 4 * half + odd:4 * half + 4:2, :],
                            b[64 * odd:64 * odd + 64, :].rearrange("p (c q) -> p c q", c=2),
                            ACT.Copy, scale=HD ** -0.5)
                elif kind == 1:
                    last = act.activation(K2[:, br, 2 * half:2 * half + 2, :],
                                          b.rearrange("p (c q) -> p c q", c=2), ACT.Copy)
                else:
                    last = act.activation(V2[:, br, half, :], b, ACT.Copy)
                last.then_inc(sem("proj2_read"), 1)

            for s in range(STICK_STEPS):
                projected2(s)
                if s == 2:
                    act.wait_ge(sem("fabs_done"), 1)
                    act.activation(fsm[:, 32:48], fsm[:, 16:32], ACT.Exp)
                    act.drain()
                    act.activation(fsm[:, 48:64], fsm[:, 32:48], ACT.Ln, bias=1.0).then_inc(sem("fln_done"), 1)

            def stick_out(p):
                act.wait_ge(sem("pv2_done"), p + 1)
                act.activation(OT[:, 0, p, :], bank(6 + p % 2, T), ACT.Copy).then_inc(sem("ot_read"), 1)

            for p in range(4):
                act.wait_ge(sem("z_done"), p + 1)
                if p:
                    act.wait_ge(sem("d_done"), p)
                act.activation(zs, ps_t[:, 1024:1024 + 768], ACT.Copy).then_inc(sem("z_read"), 1)
                act.wait_ge(sem("t_done"), p + 1)
                act.activation(te, te, ACT.Exp)
                act.drain()
                act.activation(ln1, te, ACT.Ln, bias=1.0).then_inc(sem("l_done"), 1)
                if p:
                    projected2(STICK_STEPS + 2 * p - 1)
                    stick_out(p - 1)
                projected2(STICK_STEPS + 2 * p)
                act.wait_ge(sem("d_done"), p + 1)
                if p:
                    act.wait_ge(sem("pv2_done"), p)
                act.activation(sw, te, ACT.Exp).then_inc(sem("w_done"), 1)
            projected2(STICK_STEPS + 7)
            stick_out(3)

            def exps2(u):
                act.wait_ge(sem("mx2_done"), u + 1)
                for qt in range(2):
                    c0, n = (0, P) if qt == 0 else (P, T)
                    last = act.activation(P2[:, u % 2, c0:c0 + n], P2[:, u % 2, c0:c0 + n], ACT.Exp,
                                          bias=nmax[:, 2 * (u % 4) + qt:2 * (u % 4) + qt + 1],
                                          accum_out=lsum[:, 2 * (u % 4) + qt:2 * (u % 4) + qt + 1])
                last.then_inc(sem("ex2_done"), 1)

            def pt2_out(u):
                act.wait_ge(sem("pt2_done"), u + 1)
                if u >= 4:
                    act.wait_ge(sem("pv2_done"), 4 + (u - 4) // 2 + 1)
                act.activation(PT2[:, u % 4, :], bank(4, 384), ACT.Copy).then_inc(sem("pt2_read"), 1)

            for u in range(16 + 2):
                if u < 16:
                    exps2(u)
                if 0 <= u - 1 < 16:
                    pt2_out(u - 1)
                if filler_step(u) and filler_step(u) < 26:
                    projected2(filler_step(u))
                if u >= 2 and u % 2 == 1:
                    v = (u - 3) // 2
                    act.wait_ge(sem("pv2_done"), 4 + v + 1)
                    act.activation(OT[:, 1 + v // 4, v % 4, :], bank(6 + v % 2, T),
                                   ACT.Copy).then_inc(sem("ot_read"), 1)

            act.drain()
            for n in range(2):
                for q in range(4):
                    act.activation(sig2[:, n, q, :], sig2[:, n, q, :], ACT.Sigmoid).then_inc(sem("g2_read"), 1)
            for q in range(4):
                act.wait_ge(sem("proj2_done"), 26 + q + 1)
                act.wait_ge(sem("l2_read"), q + 1)
                act.activation(sig2[:, 0, q, :], bank(q), ACT.Sigmoid).then_inc(sem("g2_read"), 1)

            norm_sums("x3_done", "ssy_done")
            norm_out("hy", V_NM2)
            for s in range(16):
                act.wait_ge(sem("up2_done"), s + 1)
                if s >= 2:
                    act.wait_ge(sem("hid_done"), s - 1)
                act.activation(relu[:, s % 2, :], bank(s % 4), ACT.Relu).then_inc(sem("up2_read"), 1)
            norm_sums("x4_done", "ssf_done")

        @block.vector
        def _(dve):
            roots = [0]

            def mean_square(dst, sums, n, eps):
                dve.tensor_scalar(dst, sums, 1.0 / n, eps, ALU.mult, ALU.add).then_inc(sem("mean_ready"), 1)

            def root():
                roots[0] += 1
                dve.wait_ge(sem("root_done"), roots[0])

            def inverse_rms(dst, sums, n, eps):
                mean_square(dst, sums, n, eps)
                root()

            dve.memset(cs_t, 0.0)
            dve.drain()
            dve.wait_ge(sem("sigc_done"), 1)
            dve.wait_ge(sem("vec_in"), 16)
            dve.tensor_tensor(cs_t[:, :, 0:2], vec[:, V_C:V_C + 16].rearrange("p (m j) -> p j m", m=2),
                              sigc.rearrange("p (m j) -> p j m", m=2), ALU.mult).then_inc(sem("cs_done"), 1)
            dve.tensor_scalar(sub08, vec[:, V_SUB:V_SUB + 1], 1.0 - LAM_INIT, None, ALU.mult)
            dve.wait_ge(sem("ss_done"), 4)
            inverse_rms(rstd[:, 0:4], ss[:, 0:4], D, EPS)
            dve.drain()
            for i in range(4):
                dve.wait_ge(sem(f"x_in{i}"), 16)
                src = xres[:, i, :] if i < 2 else ctx_in[:, i - 2, :]
                dve.tensor_scalar(xn4[:, i, :], src, rstd[:, i:i + 1], None, ALU.mult).then_inc(sem("xn_done"), 1)
            dve.wait_ge(sem("row_in"), 16)
            lprod = stat[:, 176:176 + 64]
            for i in range(2):
                dve.tensor_tensor(lprod, row[:, R_LAM + HD * i:R_LAM + HD * (i + 1)],
                                  row[:, R_LAM + 2 * HD + HD * i:R_LAM + 2 * HD + HD * (i + 1)], ALU.mult)
                dve.drain()
                dve.reduce_sum(lam2[:, i:i + 1], lprod, AX.X)
                dve.drain()
            dve.sem_inc(sem("lam_sums"), 1)

            def mod_columns(n):
                dve.wait_ge(sem("modt_done"), n + 1)
                dve.tensor_reduce(modT[:, 4 * n:4 * n + 4, :],
                                  bank(2 + n % 2).rearrange("p (q g m) -> p q g m", q=4, g=4)[:, :, :, 0:2]
                                  .rearrange("p q g m -> p q m g"), AX.X, ALU.add).then_inc(sem("modt_read"), 1)

            for n in range(4):
                mod_columns(n)
            dve.drain()

            def add_bias(c0, n):
                dve.tensor_tensor(modT[:, c0:c0 + n, :], modT[:, c0:c0 + n, :],
                                  vec[:, V_BADA + c0:V_BADA + c0 + n].unsqueeze(2).broadcast_to([P, n, 2]), ALU.add)
                dve.drain()

            add_bias(0, 16)
            dve.scalar_tensor_tensor(scale_a[:, :, :], modT[:, 8:16, :], 1.0,
                                     vec[:, V_NA:V_NA + KC].unsqueeze(2).broadcast_to([P, KC, 2]),
                                     ALU.add, ALU.mult).then_inc(sem("mod_ready"), 1)
            dve.drain()
            for j in range(1, KC, 2):
                dve.wait_ge(sem("ht_tr"), j + 1)
                for m in range(2):
                    last = dve.tensor_scalar(hT[:, j, T * m:T * m + T], bank(4 + j % 4)[:, T * m:T * m + T],
                                             scale_a[:, j, m:m + 1], modT[:, j, m:m + 1], ALU.mult, ALU.add)
                last.then_inc(sem("ht_dve"), 1)

            dve.wait_ge(sem("const_in"), 16)
            for u in range(12):
                if u < 4:
                    nh, gain, tile = 2, 1, u
                elif u < 8:
                    nh, gain, tile = 8, 3, u - 4
                elif u < 10:
                    nh, gain, tile = 8, 0, u - 8
                else:
                    nh, gain, tile = 8, 2, u - 10
                n = nh * HD
                dve.drain()
                dve.wait_ge(sem("proj_read"), (u if u < 8 else u + 4) + 1)
                src = raw[:, u % 2, 0:n].rearrange("p (h d) -> p h d", d=HD)
                g = row[:, R_GAIN + HD * gain:R_GAIN + HD * (gain + 1)].unsqueeze(1).broadcast_to([P, nh, HD])
                a = rt1[:, 0:n].rearrange("p (h d) -> p h d", d=HD)
                b = rt2[:, 0:n].rearrange("p (h d) -> p h d", d=HD)
                dve.reduce_sum(nh_ss[:, 0:nh], sq[:, u % 2, 0:n].rearrange("p (h d) -> p h d", d=HD), AX.X)
                dve.tensor_tensor(a, src, g, ALU.mult)
                dve.drain()
                mean_square(nh_rs[:, 0:nh], nh_ss[:, 0:nh], HD, EPS)
                if tile < 2:
                    cos = cst(C_ROPEC + HD * tile, HD).unsqueeze(1).broadcast_to([P, nh, HD])
                    sin = cst(C_ROPES + HD * tile, HD)
                    for k in range(2):
                        dve.tensor_tensor(b[:, :, k:HD:2], a[:, :, 1 - k:HD:2],
                                          sin[:, k:HD:2].unsqueeze(1).broadcast_to([P, nh, HD // 2]), ALU.mult)
                    dve.drain()
                    dve.tensor_tensor(a, a, cos, ALU.mult)
                    dve.drain()
                    dve.tensor_tensor(a, a, b, ALU.add)
                dve.drain()
                root()
                if u >= 2:
                    dve.wait_ge(sem("qkt_done"), u - 1)
                dve.tensor_tensor(hat[:, u % 2, 0:n].rearrange("p (h d) -> p h d", d=HD), a,
                                  nh_rs[:, 0:nh].unsqueeze(2).broadcast_to([P, nh, HD]),
                                  ALU.mult).then_inc(sem("hat_done"), 1)

            dve.wait_ge(sem("gb_in"), 32)
            for n in range(4, 12):
                if 6 <= n < 10:
                    mod_columns(n)
                else:
                    g = (g_attn if n < 6 else g_moe)[:, 512 * (n % 2):512 * (n % 2) + 512]
                    dve.wait_ge(sem("modt_done"), n + 1)
                    dve.tensor_tensor(g, bank(2 + n % 2), g, ALU.add).then_inc(sem("modt_read"), 1)
            dve.drain()
            add_bias(24, 16)
            dve.scalar_tensor_tensor(scale_m[:, :], modT[:, 32:40, 0], 1.0, vec[:, V_NM:V_NM + KC],
                                     ALU.add, ALU.mult).then_inc(sem("modm_ready"), 1)
            dve.wait_ge(sem("lam_exp"), 1)
            dve.scalar_tensor_tensor(lam, lam2[:, 0:1], LAM_INIT, lam2[:, 1:2], ALU.add, ALU.subtract)

            def maxes(n):
                dve.wait_ge(sem("sc_done"), n + 1)
                dve.reduce_max(nmax[:, n:n + 1], bank(n % 3), AX.X)
                dve.drain()
                dve.tensor_scalar(nmax[:, n:n + 1], nmax[:, n:n + 1], -1.0, None, ALU.mult).then_inc(sem("mx_done"), 1)

            def normalise(k):
                if k < 16:
                    dve.wait_ge(sem("ex_done"), k + 1)
                    dve.reciprocal(linv[:, k:k + 1], lsum[:, k:k + 1])
                    dve.drain()
                    dve.tensor_scalar(prob[:, k % 4, :], prob[:, k % 4, :], linv[:, k:k + 1], None,
                                      ALU.mult).then_inc(sem("pn_done"), 1)
                else:
                    n = 16 + 2 * (k - 16)
                    dve.wait_ge(sem("ex_done"), n + 2)
                    dve.reciprocal(linv[:, n:n + 2], lsum[:, n:n + 2])
                    dve.drain()
                    dve.tensor_scalar(prob[:, (n + 1) % 4, :], prob[:, (n + 1) % 4, :], linv[:, n + 1:n + 2],
                                      lam, ALU.mult, ALU.mult)
                    dve.drain()
                    dve.scalar_tensor_tensor(prob[:, n % 4, :], prob[:, n % 4, :], linv[:, n:n + 1],
                                             prob[:, (n + 1) % 4, :], ALU.mult, ALU.subtract).then_inc(sem("pn_done"), 1)

            def head_norm(i):
                dve.wait_ge(sem("bss_done"), i + 1)
                inverse_rms(brs[:, i:i + 1], bss[:, i:i + 1], P, SUBLN_EPS)
                dve.drain()
                if i >= 2:
                    dve.wait_ge(sem("ybt_done"), i - 1)
                dve.tensor_scalar(onorm[:, i % 2, :], bank(6 + i % 2, P), brs[:, i:i + 1], None,
                                  ALU.mult).then_inc(sem("on_done"), 1)

            maxes(0)
            for k in range(24 + 3):
                if k + 1 < 16:
                    maxes(k + 1)
                elif 16 <= k + 1 < 24:
                    maxes(16 + 2 * (k + 1 - 16))
                    maxes(17 + 2 * (k + 1 - 16))
                if k < 24:
                    normalise(k)
                if 16 <= k - 2 < 24:
                    head_norm(k - 2 - 16)
            dve.wait_ge(sem("on_done"), 8)
            for s in range(4):
                dve.wait_ge(sem("ta_done"), s + 1)
                dve.tensor_tensor(mergedT[:, 2 * s:2 * s + 2, :].rearrange("p j q -> p (j q)"), bank(s),
                                  sig[:, s, :], ALU.mult).then_inc(sem("ta_read"), 1)
            for s in range(4):
                dve.wait_ge(sem("tb_done"), s + 1)
                dve.tensor_tensor(mtmp[:, s % 2, :], bank(4 + s), sig[:, 4 + s, :], ALU.mult).then_inc(sem("tb_read"), 1)
                dve.drain()
                m = mergedT[:, 2 * s:2 * s + 2, :].rearrange("p j q -> p (j q)")
                dve.tensor_tensor(m, m, mtmp[:, s % 2, :], ALU.add).then_inc(sem("merged_done"), 1)
            for i, (hh, tt) in enumerate(((0, 0), (0, 1), (1, 0), (1, 1))):
                dve.wait_ge(sem("wo_done"), i + 1)
                cols = slice(512 * hh, 512 * hh + 512)
                dve.tensor_tensor(mtmp[:, i % 2, :], bank(i), g_attn[:, cols], ALU.mult)
                dve.drain()
                dve.tensor_tensor(xres[:, tt, cols], xres[:, tt, cols], mtmp[:, i % 2, :], ALU.add).then_inc(sem("x1_done"), 1)

            dve.wait_ge(sem("ssm_done"), 2)
            inverse_rms(rstd[:, 0:2], ss[:, 0:2], D, EPS)
            dve.drain()
            for i in range(TT):
                dve.tensor_scalar(xn2[:, i, :], xres[:, i, :], rstd[:, i:i + 1], None, ALU.mult).then_inc(sem("xm_done"), 1)
            for b in range(1, 4, 2):
                dve.wait_ge(sem("hm_tr"), b + 1)
                for j in (2 * b, 2 * b + 1):
                    last = dve.tensor_scalar(hmT[:, j, :], bank(4 + b)[:, T * (j % 2):T * (j % 2) + T],
                                             scale_m[:, j:j + 1], modT[:, 24 + j, 0:1], ALU.mult, ALU.add)
                last.then_inc(sem("hm_dve"), 1)
            BIG = 3.0e38
            dve.memset(b_all[96:128, :], 0.0)
            dve.memset(rtab, 4096.0)
            dve.memset(wtab, 0.0)
            dve.memset(logit[:, :, N_EXP:EPAD], -BIG)
            dve.wait_ge(sem("logit_done"), 1)
            dve.tensor_tensor(logit[:, :, 0:N_EXP], bank(0)[:, 0:TT * N_EXP].rearrange("p (t e) -> p t e", t=TT),
                              row[:, R_RB:R_RB + N_EXP].unsqueeze(1).broadcast_to([P, TT, N_EXP]), ALU.add)
            dve.drain()
            for i in range(TT):
                dve.max(top8[:, i, :], logit[:, i, 0:N_EXP])
            dve.drain()
            for i in range(TT):
                dve.tensor_scalar(esm[:, i:i + 1], top8[:, i, 0:1], -1.0, None, ALU.mult).then_inc(sem("top_done"), 1)
            dve.memset(top8[:, :, TOP_K:8], -BIG)
            dve.drain()
            for i in range(TT):
                dve.match_replace(out=lrep[:, i, :], in_to_replace=top8[:, i, :], in_values=logit[:, i, :],
                                  imm_value=BIG)
            dve.drain()
            dve.tensor_scalar(emask, lrep[:, :, 0:N_EXP], BIG, None, ALU.is_equal).then_inc(sem("mask_done"), 1)
            dve.drain()
            dve.wait_ge(sem("eexp_done"), 2)
            dve.tensor_tensor(wtab[:, :, 0:N_EXP], eexp, emask, ALU.mult)
            dve.drain()
            dve.reduce_sum(esm[:, 4:6], wtab[:, :, 0:N_EXP], AX.X)
            dve.drain()
            dve.reciprocal(esm[:, 6:8], esm[:, 4:6])
            dve.drain()
            dve.tensor_tensor(wtab[:, :, 0:N_EXP], wtab[:, :, 0:N_EXP],
                              esm[:, 6:8].unsqueeze(2).broadcast_to([P, TT, N_EXP]), ALU.mult)
            dve.wait_ge(sem("rank_done"), 1)
            dve.tensor_scalar(eexp, emask, -4096.0, 4096.0, ALU.mult, ALU.add)
            dve.drain()
            dve.tensor_tensor(rtab[:, :, 0:N_EXP], bank(1)[:, 0:TT * N_EXP].rearrange("p (t e) -> p t e", t=TT),
                              eexp, ALU.add)
            dve.reduce_max(esm[:, 8:9], bank(1)[:, TT * N_EXP:3 * N_EXP], AX.X)
            dve.drain()
            dve.tensor_scalar(esm[:, 9:10], esm[:, 8:9], float(CAP), 1.0, ALU.is_gt, ALU.add)
            for i in range(2, T // CAP):
                dve.drain()
                dve.scalar_tensor_tensor(esm[:, 8 + i:9 + i], esm[:, 8:9], float(CAP * i), esm[:, 7 + i:8 + i],
                                         ALU.is_gt, ALU.add)
            dve.drain()
            dve.tensor_copy(npass_t[:, :], esm[:, 7 + T // CAP:8 + T // CAP]).then_inc(sem("npass_ready"), 1)

            iota = cst(C_IOTA, CAP).unsqueeze(1).broadcast_to([P, EG, CAP])

            def select(g):
                for tt in range(TT):
                    last = dve.tensor_tensor(S4[:, tt], iota,
                                             rtab[:, tt, bass.ds(g * EG, EG)].unsqueeze(2).broadcast_to([P, EG, CAP]),
                                             ALU.is_equal)
                return last

            def expert_dve(X, it, g, gathers):
                dve.drain()
                dve.wait_ge(X["down_done"], it * EG + 1)
                for m in range(3):
                    last = dve.tensor_copy(esel[:, m], const[:, bass.ds(g * EG + (C_ID + N_EXP * m), EG)]
                                           .unsqueeze(2).broadcast_to([P, EG, CAP]))
                last.then_inc(X["sel_ready"], 1)
                for tt in range(TT):
                    last = dve.tensor_tensor(WS4[:, tt], S4[:, tt],
                                             wtab[:, tt, bass.ds(g * EG, EG)].unsqueeze(2).broadcast_to([P, EG, CAP]),
                                             ALU.mult)
                last.then_inc(X["ws4_ready"], 1)
                dve.drain()
                dve.wait_ge(X["gather_done"], gathers)
                select(g + 1).then_inc(X["s4_ready"], 1)

                def combine(n):
                    for r in range(4):
                        tt, h = r % 2, r // 2
                        dve.wait_ge(X["comb_done"], it * 8 + (1 + n + r + 1))
                        a = acc[:, tt, 512 * h:512 * h + 512]
                        dve.tensor_tensor(a, bank(6 + r % 2), a, ALU.add).then_inc(X["comb_read"], 1)

                for q in range(EG):
                    dve.wait_ge(X["gate_done"], it * EG + (q + 1))
                    dve.tensor_scalar(gbuf, bank(0), LIMIT, None, ALU.min).then_inc(X["gate_read"], 1)
                    dve.drain()
                    dve.wait_ge(X["sig_done"], it * EG + (q + 1))
                    dve.tensor_tensor(tbuf, gbuf, sbuf_, ALU.mult)
                    dve.wait_ge(X["up_done"], it * EG + (q + 1))
                    dve.tensor_scalar(ubuf, bank(1), LIMIT, -LIMIT, ALU.min, ALU.max).then_inc(X["up_read"], 1)
                    dve.drain()
                    dve.wait_ge(X["tr_done"], it * 5 + (q + 1))
                    dve.scalar_tensor_tensor(abuf.rearrange("p (c f) -> p f c", c=4),
                                             ubuf.rearrange("p (f c) -> p f c", c=4), 1.0,
                                             tbuf.rearrange("p (f c) -> p f c", c=4),
                                             ALU.add, ALU.mult).then_inc(X["act_done"], 1)
                    if q == 2:
                        combine(0)
                combine(4)
                dve.drain()

            dve.drain()
            select(0).then_inc(X1["s4_ready"], 1)
            dve.wait_ge(sem("b_all_in"), 16)
            dve.wait_ge(sem("acc_zeroed"), 1)
            for name in ("gate_read", "up_read", "comb_read"):
                dve.sem_inc(X1[name], 1)
            with dve.Fori(0, GROUPS) as it:
                expert_dve(X1, it, it, it * 4 + 4)

            def more_dve(p):
                dve.tensor_scalar(rtab, rtab, float(CAP), None, ALU.subtract)
                dve.drain()
                select(0).then_inc(X2["s4_ready"], 1)
                with dve.Fori(0, GROUPS) as g:
                    it = p * GROUPS + g
                    expert_dve(X2, it, g, it * 4 + p * 4 + 4)
            ov_passes(dve, more_dve)

            for i in range(TT):
                dve.tensor_tensor(acc[:, i, :], acc[:, i, :], g_moe[:, :], ALU.mult)
                dve.drain()
                dve.tensor_tensor(xres[:, i, :], xres[:, i, :], acc[:, i, :], ALU.add).then_inc(sem("x2_done"), 1)

            def norm_rows(sums):
                dve.wait_ge(sem(sums), 2)
                inverse_rms(rstd[:, 0:2], ss[:, 0:2], D, EPS)
                dve.drain()

            def norm_out(sums, tag, vcol):
                norm_rows(sums)
                for i in range(TT):
                    dve.tensor_scalar(xn3[:, i, :], xres[:, i, :], rstd[:, i:i + 1], None,
                                      ALU.mult).then_inc(sem(tag + "_xn"), 1)
                for b in range(1, 4, 2):
                    dve.wait_ge(sem(tag + "_tr"), b + 1)
                    for j in (2 * b, 2 * b + 1):
                        last = dve.tensor_scalar(hT2[:, j, :], bank(4 + b)[:, T * (j % 2):T * (j % 2) + T],
                                                 vec[:, vcol + j:vcol + j + 1], None, ALU.mult)
                    last.then_inc(sem(tag + "_dve"), 1)

            norm_out("ssx_done", "hx", V_NX2)
            dve.wait_ge(sem("f_done"), 1)
            dve.tensor_tensor(fsm[:, 0:16].rearrange("p (t h) -> p t h", t=TT),
                              bank(4)[:, 0:16].rearrange("p (t h) -> p t h", t=TT),
                              row[:, R_FB:R_FB + 8].unsqueeze(1).broadcast_to([P, TT, 8]), ALU.add)
            dve.drain()
            dve.scalar_tensor_tensor(fsm[:, 16:32], fsm[:, 0:16], -1.0, fsm[:, 0:16], ALU.mult, ALU.min).then_inc(sem("fabs_done"), 1)
            dve.wait_ge(sem("fln_done"), 1)
            dve.scalar_tensor_tensor(fsm[:, 64:80], fsm[:, 0:16], 0.0, fsm[:, 48:64], ALU.min, ALU.subtract)
            dve.drain()
            dve.tensor_scalar(fsm[:, 80:96], fsm[:, 64:80], -1.0, None, ALU.mult).then_inc(sem("lf_done"), 1)
            dve.wait_ge(sem("cq_done"), 1)
            dve.tensor_copy(fsm[:, 96:112], bank(5)[:, 0:16]).then_inc(sem("cq_read"), 1)

            strict = cst(C_STRICT).unsqueeze(1).broadcast_to([P, 2, P])
            addt = cst(C_ADDT).unsqueeze(1).broadcast_to([P, 2, P])

            def diagonals(a):
                return (a[:, 0:512].rearrange("p (h q) -> p h q", h=2)[:, :, 0:P],
                        a[:, 512:768].rearrange("p (h q) -> p h q", h=2))

            for p in range(4):
                dve.wait_ge(sem("z_read"), p + 1)
                if p:
                    dve.wait_ge(sem("w_done"), p)
                dve.scalar_tensor_tensor(te, zs, -1.0, zs, ALU.mult, ALU.min).then_inc(sem("t_done"), 1)
                dve.wait_ge(sem("l_done"), p + 1)
                if p:
                    dve.wait_ge(sem("s_done"), p)
                dve.scalar_tensor_tensor(sp, zs, 0.0, ln1, ALU.max, ALU.add)
                dve.drain()
                for d in diagonals(sp):
                    last = dve.tensor_tensor(d, d, strict, ALU.mult)
                last.then_inc(sem("sp_done"), 1)
                dve.wait_ge(sem("s_done"), p + 1)
                dve.tensor_tensor(te, zs, ps_t[:, 2048:2048 + 768], ALU.subtract).then_inc(sem("s_read"), 1)
                dve.drain()
                for d in diagonals(te):
                    last = dve.tensor_tensor(d, d, addt, ALU.add)
                last.then_inc(sem("d_done"), 1)

            zmask = const[:, C_ZERO:C_ZERO + T]

            def scores2(u):
                cm = CM[:, u % 2]
                if u < 8:
                    dve.wait_ge(sem("cb_done"), u + 1)
                    for qt in range(2):
                        c0, n = (0, P) if qt == 0 else (P, T)
                        last = dve.scalar_tensor_tensor(
                            cm[:, c0:c0 + n], bank(5)[:, 0:n], fsm[:, 96 + 8 * qt + u:97 + 8 * qt + u],
                            zmask[:, P:T] if qt == 0 else zmask, ALU.add, ALU.add)
                    last.then_inc(sem("cb_read"), 1)
                else:
                    slope = 2.0 ** (-8.0 * (u - 8 + 1) / HEADS2)
                    dve.scalar_tensor_tensor(cm[:, P:P + T], const[:, C_NREL:C_NREL + T], slope, zmask,
                                             ALU.mult, ALU.add)
                dve.drain()
                dve.wait_ge(sem("sc2_done"), u + 1)
                if u >= 2:
                    dve.wait_ge(sem("pt2_done"), u - 1)
                m0 = 2 * (u % 4)
                for qt in range(2):
                    c0, n = (0, P) if qt == 0 else (P, T)
                    m = cm[:, c0:c0 + n] if (u < 8 or qt) else cm[:, 2 * P:3 * P]
                    dve.tensor_tensor_reduce(out=P2[:, u % 2, c0:c0 + n], in0=bank(2 + u % 2)[:, c0:c0 + n], in1=m,
                                             scale=1.0, scalar=-3.0e38, op0=ALU.add, op1=ALU.max,
                                             accum_out=linv[:, 16 + m0 + qt:17 + m0 + qt])
                dve.drain()
                dve.tensor_scalar(nmax[:, m0:m0 + 2], linv[:, 16 + m0:18 + m0], -1.0, None,
                                  ALU.mult).then_inc(sem("mx2_done"), 1)

            def normalise2(u):
                m0 = 2 * (u % 4)
                dve.wait_ge(sem("ex2_done"), u + 1)
                dve.reciprocal(linv[:, m0:m0 + 2], lsum[:, m0:m0 + 2])
                dve.drain()
                for qt in range(2):
                    c0, n = (0, P) if qt == 0 else (P, T)
                    last = dve.tensor_scalar(P2[:, u % 2, c0:c0 + n], P2[:, u % 2, c0:c0 + n],
                                             linv[:, m0 + qt:m0 + qt + 1], None, ALU.mult)
                last.then_inc(sem("pn2_done"), 1)

            scores2(0)
            for u in range(16):
                if u + 1 < 16:
                    scores2(u + 1)
                normalise2(u)

            for n in range(3):
                for s in range(4):
                    m = mixT[:, 2 * s:2 * s + 2, :].rearrange("p j q -> p (j q)")
                    dve.wait_ge(sem("g2_read"), 4 * n + s + 1)
                    dve.wait_ge(sem("l2_done"), 4 * n + s + 1)
                    if n == 0:
                        dve.tensor_tensor(m, bank(4 + s), sig2[:, n % 2, s, :], ALU.mult).then_inc(sem("l2_read"), 1)
                    else:
                        dve.tensor_tensor(mt2, bank(4 + s), sig2[:, n % 2, s, :], ALU.mult).then_inc(sem("l2_read"), 1)
                        dve.drain()
                        dve.tensor_tensor(m, m, mt2, ALU.add)
                        dve.drain()
            dve.drain()
            dve.sem_inc(sem("mix_done"), 1)
            for i, (hh, tt) in enumerate(((0, 0), (0, 1), (1, 0), (1, 1))):
                dve.wait_ge(sem("wo2_done"), i + 1)
                xx = xres[:, tt, 512 * hh:512 * hh + 512]
                last = dve.tensor_tensor(xx, bank(i), xx, ALU.add)
                if hh == 1:
                    last.then_inc(sem("x3_done"), 1)
            norm_out("ssy_done", "hy", V_NM2)
            for s in range(16):
                dve.wait_ge(sem("up2_read"), s + 1)
                dve.tensor_tensor(hid[:, 2 * s:2 * s + 2, :].rearrange("p j q -> p (j q)"), relu[:, s % 2, :],
                                  relu[:, s % 2, :], ALU.mult).then_inc(sem("hid_done"), 1)
            for i in range(4):
                tt, hh = i // 2, i % 2
                dve.wait_ge(sem("down2_done"), 1)
                xx = xres[:, tt, 512 * hh:512 * hh + 512]
                last = dve.tensor_tensor(xx, bank(4 + i), xx, ALU.add)
                if hh == 1:
                    last.then_inc(sem("x4_done"), 1)
            norm_rows("ssf_done")
            dve.wait_ge(sem("nf_in"), 16)
            for i in range(TT):
                dve.scalar_tensor_tensor(yout[:, i, :], xres[:, i, :], rstd[:, i:i + 1], g_attn[:, :],
                                         ALU.mult, ALU.mult).then_inc(sem("y_done"), 1)

        @block.tensor
        def _(pe):
            def ready(i):
                pe.wait_ge(loaded[i % RING], 16 * (i // RING + 1))

            owed = [False]

            def used():
                owed[0] = True

            def tell_used(first):
                if owed[0]:
                    first.then_inc(block_used, 1)
                owed[0] = False

            def product(dst, terms):
                for k, (a, b) in enumerate(terms):
                    last = pe.matmul(dst, a, b, start=k == 0, stop=k == len(terms) - 1)
                    if k == 0 and len(terms) > 1:
                        tell_used(last)
                return last

            def ada(n, i):
                ready(i)
                if n >= 2:
                    pe.wait_ge(sem("modp_done"), n - 1)
                w = wq_view(i)
                for c in range(2):
                    for g in range(4):
                        last = pe.matmul(bank(n % 2)[32 * g:32 * g + 32, :], cs_t[:, 2 * g + c, :],
                                         w[:, 2 * g + c, :], start=c == 0, stop=c == 1)
                        tell_used(last)
                last.then_inc(sem("ada_done"), 1)
                used()

            def mod_transpose(n):
                pe.wait_ge(sem("modp_done"), n + 1)
                if n >= 2:
                    pe.wait_ge(sem("modt_read"), n - 1)
                for q in range(4):
                    last = pe.transpose(bank(2 + n % 2)[:, P * q:P * q + P], modp[:, n % 2, P * q:P * q + P], ident)
                last.then_inc(sem("modt_done"), 1)

            def mod_rows(n):
                pe.wait_ge(sem("modp_done"), n + 1)
                pe.wait_ge(sem("modt_read"), n - 1)
                pe.matmul(bank(2 + n % 2), const[:, C_ROW0:C_ROW0 + 1].broadcast_to([P, P]), modp[:, n % 2, :],
                          start=True, stop=True).then_inc(sem("modt_done"), 1)

            pe.wait_ge(sem("cs_done"), 1)
            pe.wait_ge(sem("const_in"), 16)
            for n in range(4):
                ada(n, W_ADA1 + n)
                if n:
                    mod_transpose(n - 1)
            mod_transpose(3)

            pe.wait_ge(sem("xn_done"), 4)
            for j in range(KC):
                if j >= 4:
                    pe.wait_ge(sem("ht_dve" if j % 2 else "ht_act"), j // 2 - 1)
                for i in range(4):
                    last = pe.transpose(bank(4 + j % 4)[:, P * i:P * i + P], xn4[:, i, P * j:P * j + P], ident)
                last.then_inc(sem("ht_tr"), 1)
            pe.wait_ge(sem("ht_act"), KC // 2)
            pe.wait_ge(sem("ht_dve"), KC // 2)

            def qk_transpose(u):
                pe.wait_ge(sem("hat_done"), u + 1)
                if u >= 4:
                    pe.wait_ge(sem("qkt_read"), u - 3)
                for c in range(1 if u < 4 else 4):
                    last = pe.transpose(bank(4 + u % 4)[:, P * c:P * c + P], hat[:, u % 2, P * c:P * c + P], ident)
                last.then_inc(sem("qkt_done"), 1)

            steps = [(W_KVA, 256, i) for i in range(4)] + [(W_KB, 512, i) for i in range(4)]
            steps += [(W_VB, 512, i) for i in range(4)] + [(W_QA, 512, i) for i in range(2)]
            steps += [(W_QB, 512, i) for i in range(2)]
            UNIT = [0, 1, 2, 3, 4, 5, 6, 7, None, None, None, None, 8, 9, 10, 11]
            pe.wait_ge(sem("modt_read"), 4)
            for s in range(24):
                if s >= 4:
                    pe.wait_ge(sem("proj_read"), s - 3)
                dst = bank(s % 4)
                if s < 16:
                    i, cols, tile = steps[s]
                    ready(i)
                    w = wq_view(i, cols)
                    last = product(dst[:, 0:cols], [(hT[:, j, P * tile:P * tile + P], w[:, j, :]) for j in range(KC)])
                    if s == 15 or steps[s + 1][0] != i:
                        used()
                else:
                    i, part = W_GATE + (s - 16) // 2, (s - 16) % 2
                    ready(i)
                    w = wq_view(i)
                    for c in range(2):
                        c0 = T * part + P * c
                        last = product(dst[:, T * c:T * c + T],
                                       [(w[:, j, c0:c0 + P], hT[:, j, 0:T]) for j in range(KC)])
                    if part == 1:
                        used()
                last.then_inc(sem("proj_done"), 1)
                if 2 <= s < 18 and UNIT[s - 2] is not None:
                    qk_transpose(UNIT[s - 2])
            pe.wait_ge(sem("proj_read"), 24)
            for n in range(4, 12):
                ada(n, W_ADA2 + n - 4)
                if n > 4:
                    (mod_transpose if 6 <= n - 1 < 10 else mod_rows)(n - 1)
            mod_rows(11)

            def scores(n):
                if n >= 3:
                    pe.wait_ge(sem("ex_done"), n - 2)
                if n < 16:
                    pe.matmul(bank(n % 3), QA[:, n // 2, P * (n % 2):P * (n % 2) + P], KTA, start=True,
                              stop=True).then_inc(sem("sc_done"), 1)
                else:
                    h, qt, m = (n - 16) // 4, ((n - 16) // 2) % 2, n % 2
                    pe.matmul(bank(n % 3), QB[:, 2 * h + m, P * qt:P * qt + P], KTB[:, h, :], start=True,
                              stop=True).then_inc(sem("sc_done"), 1)

            pe.wait_ge(sem("qkt_read"), 12)
            pe.wait_ge(sem("modp_done"), 12)
            pe.wait_ge(sem("modt_read"), 12)
            issued = 0

            def weighted_a(c):
                pe.wait_ge(sem("pt_read"), 4 * c + 4)
                if c >= 2:
                    pe.wait_ge(sem("ya_read"), c - 1)
                g = c // 2
                for kc in range(4):
                    for hh in range(2):
                        last = pe.matmul(bank(6 + c % 2, T)[64 * hh:64 * hh + 64, :], VA[:, kc, 64 * g:64 * g + 64],
                                         PTA[:, 2 * (c % 2) + hh, kc, :], start=kc == 0, stop=kc == 3)
                last.then_inc(sem("pv_done"), 1)

            def weighted_b(i):
                pe.wait_ge(sem("pt_read"), 16 + i + 1)
                if i < 2:
                    pe.wait_ge(sem("ya_read"), 3 + i)
                else:
                    pe.wait_ge(sem("on_done"), i - 1)
                h = i // 2
                product(bank(6 + i % 2, P), [(PTB[:, i % 4, kc, :], VB[:, kc, P * h:P * h + P])
                                             for kc in range(4)]).then_inc(sem("pv_done"), 1)

            def yb_transpose(i):
                pe.wait_ge(sem("on_done"), i + 1)
                if i:
                    pe.wait_ge(sem("ybt_read"), i)
                pe.transpose(bank(3, P), onorm[:, i % 2, :], ident).then_inc(sem("ybt_done"), 1)

            for k in range(24 + 3):
                last_n = k if k < 16 else 17 + 2 * (k - 16)
                while issued < min(last_n + 3, 32):
                    scores(issued)
                    issued += 1
                if k < 24:
                    pe.wait_ge(sem("pn_done"), k + 1)
                    if k >= 2:
                        pe.wait_ge(sem("pt_read"), k - 1)
                    n = k if k < 16 else 16 + 2 * (k - 16)
                    for kc in range(4):
                        last = pe.transpose(bank(4 + k % 2)[:, P * kc:P * kc + P],
                                            prob[:, n % 4, P * kc:P * kc + P], ident)
                    last.then_inc(sem("pt_done"), 1)
                if 0 <= k - 1 < 16 and (k - 1) % 4 == 3:
                    weighted_a((k - 1) // 4)
                if 16 <= k - 1 < 24:
                    weighted_b(k - 1 - 16)
                if 16 <= k - 2 < 24:
                    yb_transpose(k - 2 - 16)

            pe.wait_ge(sem("ya_read"), 4)
            pe.wait_ge(sem("ybt_read"), 8)
            pe.wait_ge(sem("ex_done"), 32)
            pe.wait_ge(sem("on_done"), 8)
            for base, i, src, name in ((0, W_OA, yaT, "ta_done"), (4, W_OB, ybT, "tb_done")):
                ready(i)
                w = w4_view(i)
                for s in range(4):
                    for c in range(2):
                        c0 = T * s + P * c
                        last = product(bank(base + s)[:, T * c:T * c + T],
                                       [(w[:, k, c0:c0 + P], src[:, k, :]) for k in range(4)])
                    if s == 3:
                        used()
                    last.then_inc(sem(name), 1)

            def out_product(srcT, first, read, done):
                for hh in range(2):
                    ready(first + hh)
                    w = wq_view(first + hh)
                    for tt in range(TT):
                        last = product(bank(2 * hh + tt), [(srcT[:, j, P * tt:P * tt + P], w[:, j, :]) for j in range(KC)])
                        if tt == 1:
                            used()
                        last.then_inc(sem(done), 1)

            pe.wait_ge(sem("ta_read"), 4)
            pe.wait_ge(sem("merged_done"), 4)
            out_product(mergedT, W_OUT, None, "wo_done")

            def norm_transpose(src, xn, tag):
                pe.wait_ge(sem(xn), 2)
                for j in range(KC):
                    for i in range(TT):
                        last = pe.transpose(bank(4 + j // 2)[:, T * (j % 2) + P * i:T * (j % 2) + P * i + P],
                                            src[:, i, P * j:P * j + P], ident)
                    if j % 2:
                        last.then_inc(sem(tag + "_tr"), 1)

            norm_transpose(xn2, "xm_done", "hm")
            pe.wait_ge(sem("hm_act"), 2)
            pe.wait_ge(sem("hm_dve"), 2)
            pe.wait_ge(sem("rw_in"), 16)
            pe.wait_ge(sem("x1_done"), 4)
            for tt in range(TT):
                last = product(bank(0)[:, N_EXP * tt:N_EXP * (tt + 1)],
                               [(hmT[:, j, P * tt:P * tt + P], rw[:, j, :]) for j in range(KC)])
            last.then_inc(sem("logit_done"), 1)
            for i in range(4):
                tt, half = i // 2, i % 2
                for jj in range(4):
                    last = pe.transpose(bank(4 + i)[:, P * jj:P * jj + P],
                                        hmT[:, 4 * half + jj, P * tt:P * tt + P], ident)
                last.then_inc(sem("hp_tr"), 1)
            pe.wait_ge(sem("mask_done"), 1)
            ones, strict = cst(C_ONES), cst(C_STRICT)
            product(bank(1)[:, 0:N_EXP], [(strict, emask[:, 0, :])])
            product(bank(1)[:, N_EXP:2 * N_EXP], [(ones, emask[:, 0, :]), (strict, emask[:, 1, :])])
            product(bank(1)[:, 2 * N_EXP:3 * N_EXP], [(ones, emask[:, 0, :]), (ones, emask[:, 1, :])]
                    ).then_inc(sem("rank_done"), 1)

            def gather(X, n, s4):
                pe.wait_ge(X["s4_ready"], s4)
                for r in range(4):
                    if r >= 2:
                        pe.wait_ge(X["gather_read"], n + r - 1)
                    for jj in range(2):
                        j = 2 * r + jj
                        for tt in range(TT):
                            last = pe.matmul(bank(4 + r % 2)[:, T * jj:T * jj + T], hperm[:, tt, j // 4, j % 4, :],
                                             S4[:, tt].rearrange("p e s -> p (e s)"), start=tt == 0, stop=tt == 1)
                    last.then_inc(X["gather_done"], 1)

            def expert_pe(X, it, gathers, s4, base, in_slot):
                pe.wait_ge(X["gather_read"], gathers)
                pe.wait_ge(X["ws4_ready"], it + 1)
                pe.wait_ge(X["tr_read"], it * 5 + 1)
                for pr in range(2):
                    for tt in range(TT):
                        last = pe.transpose(bank(3)[:, P * (2 * pr + tt):P * (2 * pr + tt) + P],
                                            WS4[:, tt, 2 * pr:2 * pr + 2, :].rearrange("p e s -> p (e s)"), ident)
                last.then_inc(X["tr_done"], 1)
                pe.wait_ge(X["sel_ready"], it + 1)

                def halves(dst, m, q, k, stationary):
                    for half in range(2):
                        i = base + q * BLK_EXP + 2 * m + half
                        in_slot(i, it)
                        w = w4_view(i)
                        for c in range(4):
                            for g in range(2):
                                last = pe.matmul(dst[CAP * g:CAP * g + CAP, :], stationary(half, c),
                                                 w[:, c, 512 * g:512 * g + 512], start=half == 0 and c == 0, stop=False)
                        last.then_inc(X["free"], 1)
                    for g in range(2):
                        last = pe.matmul(dst[CAP * g:CAP * g + CAP, :], esel[:, m, q, :],
                                         b_all[:, 512 * g:512 * g + 512], start=False, stop=True)
                    return last

                def combine(n, pr):
                    pe.wait_ge(X["y_read"], it * EG + (1 + 2 * pr + 2))
                    for r in range(4):
                        tt, h = r % 2, r // 2
                        if n + r >= 2:
                            pe.wait_ge(X["comb_read"], it * 8 + (1 + n + r - 1))
                        else:
                            pe.wait_ge(X["comb_read"], it * 8 + 1)
                        pe.matmul(bank(6 + r % 2), WST[:, P * (2 * pr + tt):P * (2 * pr + tt) + P],
                                  ypair[:, 512 * h:512 * h + 512], start=True, stop=True).then_inc(X["comb_done"], 1)

                for q in range(EG):
                    tokens = lambda half, c, q=q: xeT[:, 4 * half + c, CAP * q:CAP * q + CAP]
                    pe.wait_ge(X["gate_read"], it * EG + (1 + q))
                    halves(bank(0), 0, q, 0, tokens).then_inc(X["gate_done"], 1)
                    pe.wait_ge(X["up_read"], it * EG + (1 + q))
                    halves(bank(1), 1, q, 0, tokens).then_inc(X["up_done"], 1)
                    if q == 2:
                        combine(0, 0)
                    if q == EG - 1:
                        gather(X, gathers, s4)
                    pe.wait_ge(X["act_done"], it * EG + (q + 1))
                    pe.wait_ge(X["tr_read"], it * 5 + (1 + q + 1))
                    for c in range(4):
                        last = pe.transpose(bank(3)[:, P * c:P * c + P], abuf[:, P * c:P * c + P], ident)
                    last.then_inc(X["tr_done"], 1)
                    pe.wait_ge(X["tr_read"], it * 5 + (1 + q + 2))
                    pe.wait_ge(X["y_read"], it * EG + (1 + q))
                    halves(bank(2), 2, q, 0, lambda half, c: actT[:, c, half, :]).then_inc(X["down_done"], 1)
                combine(4, 1)

            pe.wait_ge(sem("b_all_in"), 16)
            pe.wait_ge(sem("hp_read"), 4)
            gather(X1, 0, 1)
            pe.wait_ge(sem("npass_ready"), 1)

            laps = EG * BLK_EXP // RING

            def slot1(i, it):
                pe.wait_ge(loaded[i % RING], it * (16 * laps) + 16 * (i // RING + 1))

            for name in ("down_done", "comb_done"):
                pe.sem_inc(X1[name], 1)
            with pe.Fori(0, GROUPS) as it:
                expert_pe(X1, it, it * 4 + 4, it + 2, W_MOE, slot1)

            def more_pe(p):
                gather(X2, p * (4 * GROUPS + 4), p * (GROUPS + 1) + 1)
                with pe.Fori(0, GROUPS) as g:
                    def slot2(i, it):
                        pe.wait_ge(X2["loaded"][i % RING],
                                   ((p - 1) * GROUPS + g) * (16 * laps) + 16 * (i // RING + 1))
                    it = p * GROUPS + g
                    expert_pe(X2, it, it * 4 + p * 4 + 4, it + p + 2, 0, slot2)
            ov_passes(pe, more_pe, lambda: pe.sem_inc(X2["free"], RING))

            norm_transpose(xn3, "hx_xn", "hx")
            pe.wait_ge(sem("hx_act"), 2)
            pe.wait_ge(sem("hx_dve"), 2)

            def by_feature(dst, w, c0, src, chunks):
                for c in range(2):
                    last = product(dst[:, T * c:T * c + T],
                                   [(w[:, j, c0 + P * c:c0 + P * c + P], src[:, j, :]) for j in range(chunks)])
                return last

            def project2(s):
                kind, half = (s // 2) % 3, s % 2
                i = W_QKV2 + s // 2
                if s >= 28:
                    pe.wait_ge(sem("mx2_done"), 16)
                elif s >= 4:
                    pe.wait_ge(sem("proj2_read"), s - 3 if s < STICK_STEPS else s - 1)
                ready(i)
                w = wq_view(i)
                b = bank(step_bank(s))
                if kind < 2 or s >= 18:
                    last = by_feature(b, w, T * half, hT2, KC)
                else:
                    last = product(b, [(hT2[:, j, P * half:P * half + P], w[:, j, :]) for j in range(KC)])
                if half:
                    used()
                last.then_inc(sem("proj2_done"), 1)

            for s in range(STICK_STEPS):
                project2(s)
                if s == 1:
                    pe.wait_ge(sem("wf_in"), 16)
                    for tt in range(TT):
                        last = product(bank(4)[:, 8 * tt:8 * tt + 8],
                                       [(hT2[:, j, P * tt:P * tt + P], wf[:, j, :]) for j in range(KC)])
                    last.then_inc(sem("f_done"), 1)
            ule = cst(C_ULE)
            pe.wait_ge(sem("lf_done"), 1)
            product(bank(5)[:, 0:8], [(ule, fsm[:, 64:72])])
            product(bank(5)[:, 8:16], [(ones, fsm[:, 64:72]), (ule, fsm[:, 72:80])]).then_inc(sem("cq_done"), 1)

            def stick_scores(p):
                if p:
                    pe.wait_ge(sem("z_read"), p)
                q = Q2[:, 0, 2 * p:2 * p + 2, :]
                pe.matmul(bank(2), K2[:, 0, p, 0:P], q, start=True, stop=True)
                pe.matmul(bank(3, T), K2[:, 0, p, P:T], q[:, :, P:T], start=True,
                          stop=True).then_inc(sem("z_done"), 1)

            pe.wait_ge(sem("proj2_read"), STICK_STEPS)
            stick_scores(0)
            suffix = cst(C_SUF)
            for p in range(4):
                project2(STICK_STEPS + 2 * p)
                if p + 1 < 4:
                    stick_scores(p + 1)
                pe.wait_ge(sem("sp_done"), p + 1)
                if p:
                    pe.wait_ge(sem("s_read"), p)
                else:
                    pe.wait_ge(sem("cq_read"), 1)
                pe.matmul(bank(4), suffix, sp[:, 0:512], start=True, stop=False)
                pe.matmul(bank(4).rearrange("p (h q) -> p h q", h=2)[:, :, P:T], ones, sp[:, 512:768],
                          start=False, stop=True)
                pe.matmul(bank(5, T), suffix, sp[:, 512:768], start=True, stop=True).then_inc(sem("s_done"), 1)
                project2(STICK_STEPS + 2 * p + 1)
                pe.wait_ge(sem("w_done"), p + 1)
                if p >= 2:
                    pe.wait_ge(sem("ot_read"), p - 1)
                for hh in range(2):
                    h = 2 * p + hh
                    pe.matmul(bank(6 + p % 2, T)[64 * hh:64 * hh + 64, :], V2[:, 0, 0, HD * h:HD * h + HD],
                              sw[:, T * hh:T * hh + T], start=True, stop=False)
                for hh in range(2):
                    h = 2 * p + hh
                    last = pe.matmul(bank(6 + p % 2, T)[64 * hh:64 * hh + 64, P:T], V2[:, 0, 1, HD * h:HD * h + HD],
                                     sw[:, 512 + P * hh:512 + P * hh + P], start=False, stop=True)
                last.then_inc(sem("pv2_done"), 1)

            def scores2(u):
                br, h = 1 + u // 8, u % 8
                if u < 8:
                    if u:
                        pe.wait_ge(sem("cb_read"), u)
                    else:
                        pe.wait_ge(sem("s_read"), 4)
                        pe.wait_ge(sem("z_read"), 4)
                    neg = [fsm[:, 80 + 8 * tt + h:81 + 8 * tt + h].broadcast_to([P, P]) for tt in range(TT)]
                    pe.matmul(bank(5, T), neg[0], const[:, C_ULE:C_ULE + T], start=True, stop=False)
                    pe.matmul(bank(5)[:, P:T], neg[1], ule, start=False, stop=True).then_inc(sem("cb_done"), 1)
                if u >= 2:
                    pe.wait_ge(sem("mx2_done"), u - 1)
                if h == 0:
                    pe.wait_ge(sem("proj2_read"), 6 * br + 4)
                k = K2[:, br, h // 2, :]
                pe.matmul(bank(2 + u % 2)[:, 0:P], Q2[:, br, h, 0:P], k[:, 0:P], start=True, stop=True)
                pe.matmul(bank(2 + u % 2)[:, P:P + T], Q2[:, br, h, P:T], k, start=True,
                          stop=True).then_inc(sem("sc2_done"), 1)

            def weighted2(v):
                pe.wait_ge(sem("pt2_read"), 2 * v + 2)
                pe.wait_ge(sem("ot_read"), 4 + v - 1)
                br = 1 + v // 4
                if v % 4 == 0:
                    pe.wait_ge(sem("proj2_read"), 6 * br + 6)
                for kc in range(2):
                    for hh in range(2):
                        h = 2 * (v % 4) + hh
                        pt = PT2[:, (2 * v + hh) % 4, :]
                        dst = bank(6 + v % 2, T)[64 * hh:64 * hh + 64, :]
                        last = pe.matmul(dst if kc == 0 else dst[:, P:T], V2[:, br, kc, HD * h:HD * h + HD],
                                         pt[:, 0:T] if kc == 0 else pt[:, T:T + P], start=kc == 0, stop=kc == 1)
                last.then_inc(sem("pv2_done"), 1)

            scores2(0)
            for u in range(16):
                if u + 1 < 16:
                    scores2(u + 1)
                if filler_step(u):
                    project2(filler_step(u))
                pe.wait_ge(sem("pn2_done"), u + 1)
                if u:
                    pe.wait_ge(sem("pt2_read"), u)
                for d0, s0 in ((0, 0), (P, P), (2 * P, 2 * P)):
                    last = pe.transpose(bank(4)[:, d0:d0 + P], P2[:, u % 2, s0:s0 + P], ident)
                last.then_inc(sem("pt2_done"), 1)
                if u >= 2 and u % 2 == 0:
                    weighted2(u // 2 - 1)
            project2(28)
            weighted2(7)
            project2(29)

            pe.wait_ge(sem("pt2_read"), 16)
            pe.wait_ge(sem("ot_read"), 12)
            for n in range(3):
                ready(W_BR2 + n)
                for s in range(4):
                    if n:
                        pe.wait_ge(sem("l2_read"), 4 * (n - 1) + s + 1)
                    last = by_feature(bank(4 + s), w4_view(W_BR2 + n), T * s, OT[:, n], 4)
                    if s == 3:
                        used()
                    last.then_inc(sem("l2_done"), 1)
            pe.wait_ge(sem("g2_read"), 12)
            pe.wait_ge(sem("mix_done"), 1)
            out_product(mixT, W_OUT2, None, "wo2_done")

            norm_transpose(xn3, "hy_xn", "hy")
            pe.wait_ge(sem("hy_act"), 2)
            pe.wait_ge(sem("hy_dve"), 2)
            for s in range(16):
                i = W_UP2 + s // 2
                ready(i)
                if s < 4:
                    pe.wait_ge(sem("x3_done"), 2)
                else:
                    pe.wait_ge(sem("up2_read"), s - 3)
                last = by_feature(bank(s % 4), wq_view(i), T * (s % 2), hT2, KC)
                if s % 2:
                    used()
                last.then_inc(sem("up2_done"), 1)
            for i in range(8):
                ready(W_DOWN2 + i)
                pe.wait_ge(sem("hid_done"), 2 * i + 2)
                w = w4_view(W_DOWN2 + i)
                for c in range(4):
                    for tt in range(TT):
                        for hh in range(2):
                            last = pe.matmul(bank(4 + 2 * tt + hh), hid[:, 4 * i + c, P * tt:P * tt + P],
                                             w[:, c, 512 * hh:512 * hh + 512], start=i == 0 and c == 0,
                                             stop=i == 7 and c == 3)
                            tell_used(last)
                if i < 7:
                    last.then_inc(block_used, 1)
            last.then_inc(sem("down2_done"), 1)


def launch_arrays(inp):
    a = lambda n: np.asarray(inp[n])
    parts = lambda v: v.reshape(-1, P).T
    vec = np.concatenate([parts(a("c")[0]), parts(a("c_ctx")), parts(a("b_ada")[0]), parts(a("norm_attn")[0]),
                          parts(a("norm_mlp")[0]), parts(a("norm_mix_2")[0]), parts(a("norm_mlp_2")[0]),
                          parts(a("subln_b")[0])], axis=1)
    row = np.concatenate([a(n)[0] for n in ("q_norm_a", "k_norm_a", "q_norm_b", "k_norm_b", "lambda_q1",
                                            "lambda_q2", "lambda_k1", "lambda_k2", "router_b", "b_forget_2")])
    w_in_2 = a("w_in_2")[0]
    by_chunk = lambda w: w.reshape(KC, P, -1).transpose(1, 0, 2).reshape(P, -1)
    return {
        "const": constants(), "vec": vec, "row": row[None, :], "b_ada": a("b_ada"),
        "norm_final": a("norm_final_2")[None, :],
        "x": a("x")[0], "ctx": a("ctx")[0], "w_ada": a("w_ada")[0], "w_in": a("w_in")[0], "w_oa": a("w_oa")[0],
        "w_ob": a("w_ob")[0], "w_out": a("w_out")[0], "router_w": by_chunk(a("router_w")[0]),
        "w_gate": a("w_gate")[0], "w_up": a("w_up")[0], "w_down": a("w_down")[0],
        "b_all": np.concatenate([a("b_gate")[0], a("b_up")[0], a("b_down")[0]]),
        "w_in_2": w_in_2, "w_forget": by_chunk(w_in_2[:, 3072:3080]), "w_branch_2": a("w_branch_2")[0],
        "w_out_2": a("w_out_2")[0], "w_up_2": a("w_up_2")[0], "w_down_2": a("w_down_2")[0],
    }


def kernel(**inputs):
    import concourse.bacc as bacc
    from concourse.bass_utils import run_bass_kernel_spmd

    nc = bacc.Bacc("TRN2", target_bir_lowering=False, num_devices=1)
    arrays, aps = {}, {}
    for name, a in launch_arrays(inputs).items():
        a = np.ascontiguousarray(a)
        arrays[f"in_{name}"] = a
        aps[name] = nc.dram_tensor(f"in_{name}", a.shape, F32, kind="ExternalInput").ap()
    out = nc.dram_tensor("out_x", (T, D), F32, kind="ExternalOutput").ap()
    two_blocks(nc, aps, out)
    r = run_bass_kernel_spmd(nc, [arrays], core_ids=[0])
    return np.asarray(r.results[0]["out_x"]).reshape(1, T, D)
```
